# Optimizing a Trainium2 kernel written in Bass

```python
import jax
import jax.numpy as jnp
from jax import lax
import numpy as np
import jax, jax.numpy as jnp

D_MODEL = 1024
BATCH = 1
SEQ = 256
DEPTH = 1

D_MIX = D_MODEL
D_POOL = D_MIX // 2
D_ATTN = D_MIX - D_POOL
POOL_WINDOWS = (2, 4, 8, 16)
N_POOL_GROUPS = len(POOL_WINDOWS)
POOL_GROUP_DIM = D_POOL // N_POOL_GROUPS
HEAD_DIM = 64
N_HEADS = D_ATTN // HEAD_DIM
DILATION_PAIRS = ((128, 1), (512, 4), (2048, 16))
Q_BLOCK = 128
D_PROJ_IN = D_POOL + 3 * D_ATTN
D_FF = 2816
N_MOD = 9
EPS = 1e-6


def rmsnorm(x, g):
    xf = x.astype(jnp.float32)
    y = xf * lax.rsqrt(jnp.mean(xf * xf, axis=-1, keepdims=True) + EPS)
    return (y * g.astype(jnp.float32)).astype(x.dtype)

def modulate(n, shift, scale):
    return n * (1 + scale) + shift

def swiglu(n, w_gate, w_up, w_down):
    return (jax.nn.silu(n @ w_gate) * (n @ w_up)) @ w_down

def alibi_slopes(n_heads):
    return jnp.exp2(-8.0 * jnp.arange(1, n_heads + 1, dtype=jnp.float32) / n_heads)

def multiscale_pool(u, w_pool, pool_scale):
    B, S, C = u.shape
    uf = u.astype(jnp.float32)
    cs0 = jnp.pad(jnp.cumsum(uf, axis=1), ((0, 0), (1, 0), (0, 0)))
    t = jnp.arange(S)
    groups = []
    for g, w in enumerate(POOL_WINDOWS):
        sl = slice(g * POOL_GROUP_DIM, (g + 1) * POOL_GROUP_DIM)
        csg = cs0[..., sl]
        lower = jnp.pad(csg[:, :S + 1 - w], ((0, 0), (w - 1, 0), (0, 0)))
        count = jnp.minimum(t + 1, w).astype(jnp.float32)[None, :, None]
        mean = (csg[:, 1:] - lower) / count
        groups.append(mean - uf[..., sl])
    pooled = jnp.stack(groups, axis=2)
    y = jnp.einsum('bsgc,gcd->bsgd', pooled, w_pool.astype(jnp.float32)).reshape(B, S, C)
    return (y * pool_scale.astype(jnp.float32)).astype(u.dtype)

def dilated_attention(q, k, v):
    B, S, H, Dh = q.shape
    n_blk = S // Q_BLOCK
    slopes = alibi_slopes(H)
    scale = Dh ** -0.5

    def block(i):
        t0 = i * Q_BLOCK
        t = t0 + jnp.arange(Q_BLOCK)
        qb = lax.dynamic_slice_in_dim(q, t0, Q_BLOCK, axis=1).astype(jnp.float32) * scale
        mxs, dens, nums = [], [], []
        for window, dil in DILATION_PAIRS:
            dist = dil * jnp.arange(window // dil + 1)
            idx = t[:, None] - dist[None, :]
            valid = idx >= 0
            idx = jnp.maximum(idx, 0)
            kg = jnp.take(k, idx, axis=1).astype(jnp.float32)
            vg = jnp.take(v, idx, axis=1).astype(jnp.float32)
            s = jnp.einsum('bqhd,bqjhd->bqhj', qb, kg)
            s = s - slopes[:, None] * dist.astype(jnp.float32)[None, :]
            s = jnp.where(valid[None, :, None, :], s, -jnp.inf)
            mx = jnp.max(s, axis=-1)
            p = jnp.exp(s - mx[..., None])
            dens.append(jnp.sum(p, axis=-1))
            nums.append(jnp.einsum('bqhj,bqjhd->bqhd', p, vg))
            mxs.append(mx)
        m_all = jnp.stack(mxs)
        w_r = jnp.exp(m_all - jnp.max(m_all, axis=0))
        num = sum(w_r[r][..., None] * nums[r] for r in range(len(DILATION_PAIRS)))
        den = sum(w_r[r] * dens[r] for r in range(len(DILATION_PAIRS)))
        return (num / den[..., None]).astype(q.dtype)

    out = lax.map(block, jnp.arange(n_blk))
    return jnp.moveaxis(out, 0, 1).reshape(B, S, H, Dh)

def hybrid_mixer(n, w_in, w_pool, pool_scale, w_out):
    B, S, _ = n.shape
    z = n @ w_in
    u, q, k, v = jnp.split(z, [D_POOL, D_POOL + D_ATTN, D_POOL + 2 * D_ATTN], axis=-1)
    y_pool = multiscale_pool(u, w_pool, pool_scale)
    hs = (B, S, N_HEADS, HEAD_DIM)
    y_attn = dilated_attention(q.reshape(hs), k.reshape(hs), v.reshape(hs)).reshape(B, S, D_ATTN)
    return jnp.concatenate([y_pool, y_attn], axis=-1) @ w_out

def first_inputs(seed: int = 0) -> dict:
    key = jax.random.key(seed)
    ks = jax.random.split(key, 20)
    f32 = jnp.float32
    L, D = DEPTH, D_MODEL

    def nrm(k, shape, fan_in, mult=1.0):
        return jax.random.normal(k, shape, f32) * (mult * fan_in ** -0.5)

    def gain(k, shape):
        return 1.0 + 0.05 * jax.random.normal(k, shape, f32)

    return {
        "x": jax.random.normal(ks[0], (BATCH, SEQ, D), f32),
        "c": jax.random.normal(ks[1], (BATCH, D), f32),
        "w_ada": nrm(ks[2], (L, D, N_MOD * D), D, 0.5),
        "b_ada": 0.02 * jax.random.normal(ks[3], (L, N_MOD * D), f32),
        "g_ffn1": gain(ks[4], (L, D)),
        "w1_gate": nrm(ks[5], (L, D, D_FF), D),
        "w1_up": nrm(ks[6], (L, D, D_FF), D),
        "w1_down": nrm(ks[7], (L, D_FF, D), D_FF),
        "g_mix": gain(ks[8], (L, D)),
        "w_in": nrm(ks[9], (L, D, D_PROJ_IN), D),
        "w_pool": nrm(ks[10], (L, N_POOL_GROUPS, POOL_GROUP_DIM, POOL_GROUP_DIM), POOL_GROUP_DIM),
        "pool_scale": gain(ks[11], (L, D_POOL)),
        "w_out": nrm(ks[12], (L, D_MIX, D), D_MIX),
        "g_ffn2": gain(ks[13], (L, D)),
        "w2_gate": nrm(ks[14], (L, D, D_FF), D),
        "w2_up": nrm(ks[15], (L, D, D_FF), D),
        "w2_down": nrm(ks[16], (L, D_FF, D), D_FF),
        "g_final": gain(ks[17], (D,)),
    }

def first_block(x, c, w_ada, b_ada, g_ffn1, w1_gate, w1_up, w1_down, g_mix, w_in, w_pool,
              pool_scale, w_out, g_ffn2, w2_gate, w2_up, w2_down, g_final):
    h = x
    for l in range(DEPTH):
        mod = (jax.nn.silu(c) @ w_ada[l] + b_ada[l])[:, None, :]
        sh1, sc1, gt1, sh2, sc2, gt2, sh3, sc3, gt3 = jnp.split(mod, N_MOD, axis=-1)
        n = modulate(rmsnorm(h, g_ffn1[l]), sh1, sc1)
        h = h + 0.5 * gt1 * swiglu(n, w1_gate[l], w1_up[l], w1_down[l])
        n = modulate(rmsnorm(h, g_mix[l]), sh2, sc2)
        h = h + gt2 * hybrid_mixer(n, w_in[l], w_pool[l], pool_scale[l], w_out[l])
        n = modulate(rmsnorm(h, g_ffn2[l]), sh3, sc3)
        h = h + 0.5 * gt3 * swiglu(n, w2_gate[l], w2_up[l], w2_down[l])
    return rmsnorm(h, g_final)


DEPTH_2 = 2

N_MIXERS = 2
N_HEADS_2 = D_MODEL // HEAD_DIM
MIX_WIDTH = N_HEADS_2 * HEAD_DIM
N_KV_A = max(1, N_HEADS_2 // 8)
N_KV_B = max(1, N_HEADS_2 // 4)
WINDOW = 128
MOBA_BLOCK = 256
MOBA_TOPK = 3
MOBA_Q_CHUNK = 16
ROPE_THETA = 10000.0
NORM_EPS = 1e-5
NEG = -1e30
N_LAYERS_A = (DEPTH_2 + 1) // 2
N_LAYERS_B = DEPTH_2 // 2
IN_A = 2 * MIX_WIDTH + 2 * N_KV_A * HEAD_DIM
IN_B = 2 * MIX_WIDTH + 2 * N_KV_B * HEAD_DIM


def rmsnorm_2(x, g):
    xf = x.astype(jnp.float32)
    y = xf * lax.rsqrt(jnp.mean(xf * xf, axis=-1, keepdims=True) + NORM_EPS)
    return (y * g.astype(jnp.float32)).astype(x.dtype)

def rope_tables(seq):
    pos = jnp.arange(seq, dtype=jnp.float32)
    inv = ROPE_THETA ** (-jnp.arange(0, HEAD_DIM, 2, dtype=jnp.float32) / HEAD_DIM)
    ang = pos[:, None] * inv[None, :]
    return jnp.cos(ang), jnp.sin(ang)

def apply_rope(x, cos, sin):
    half = HEAD_DIM // 2
    x1, x2 = x[..., :half], x[..., half:]
    c, s = cos[None, :, None, :], sin[None, :, None, :]
    out = jnp.concatenate([x1 * c - x2 * s, x2 * c + x1 * s], axis=-1)
    return out.astype(x.dtype)

def split_proj(h, w_in, n_kv):
    B, S, _ = h.shape
    proj = h @ w_in
    kvw = n_kv * HEAD_DIM
    q = proj[..., :MIX_WIDTH].reshape(B, S, N_HEADS_2, HEAD_DIM)
    k = proj[..., MIX_WIDTH:MIX_WIDTH + kvw].reshape(B, S, n_kv, HEAD_DIM)
    v = proj[..., MIX_WIDTH + kvw:MIX_WIDTH + 2 * kvw].reshape(B, S, n_kv, HEAD_DIM)
    z = proj[..., MIX_WIDTH + 2 * kvw:]
    return q, k, v, z

def sliding_window_sink_attention(q, k, v, sinks):
    B, S, H, d = q.shape
    kvh = k.shape[2]
    G = H // kvh
    nq = S // WINDOW
    scale = 1.0 / np.sqrt(d)
    qb = q.reshape(B, nq, WINDOW, kvh, G, d)
    pad = ((0, 0), (WINDOW, 0), (0, 0), (0, 0))
    kb = jnp.pad(k, pad).reshape(B, nq + 1, WINDOW, kvh, d)
    vb = jnp.pad(v, pad).reshape(B, nq + 1, WINDOW, kvh, d)
    kband = jnp.concatenate([kb[:, :-1], kb[:, 1:]], axis=2)
    vband = jnp.concatenate([vb[:, :-1], vb[:, 1:]], axis=2)
    s = jnp.einsum('bnikgd,bnjkd->bnkgij', qb, kband).astype(jnp.float32) * scale
    i = jnp.arange(WINDOW)[:, None]
    j = jnp.arange(2 * WINDOW)[None, :]
    band = (j > i) & (j <= i + WINDOW)
    not_pad = (jnp.arange(nq)[:, None, None] > 0) | (j[None] >= WINDOW)
    mask = band[None] & not_pad
    s = jnp.where(mask[None, :, None, None], s, NEG)
    sink = jnp.broadcast_to(sinks.astype(jnp.float32).reshape(kvh, G)[None, None, :, :, None, None],
                            s.shape[:-1] + (1,))
    p = jax.nn.softmax(jnp.concatenate([s, sink], axis=-1), axis=-1)[..., :-1]
    o = jnp.einsum('bnkgij,bnjkd->bnikgd', p.astype(v.dtype), vband)
    return o.reshape(B, S, H, d)

def moba_attention(q, k, v):
    B, S, H, d = q.shape
    kvh = k.shape[2]
    G = H // kvh
    nb = -(-S // MOBA_BLOCK)
    Sp = nb * MOBA_BLOCK
    scale = 1.0 / np.sqrt(d)
    pad = ((0, 0), (0, Sp - S), (0, 0), (0, 0))
    kblk = jnp.pad(k, pad).reshape(B, nb, MOBA_BLOCK, kvh, d).transpose(0, 3, 1, 2, 4)
    vblk = jnp.pad(v, pad).reshape(B, nb, MOBA_BLOCK, kvh, d).transpose(0, 3, 1, 2, 4)
    kmean = jnp.mean(kblk.astype(jnp.float32), axis=3)
    qg = q.reshape(B, S, kvh, G, d)
    gate = jnp.einsum('bskgd,bknd->bskgn', qg.astype(jnp.float32), kmean)
    qblock = jnp.arange(S) // MOBA_BLOCK
    past = jnp.arange(nb)[None, :] < qblock[:, None]
    gate = jnp.where(past[None, :, None, None, :], gate, NEG)
    kk = min(MOBA_TOPK, nb)
    _, idx = lax.top_k(gate, kk)
    nc = S // MOBA_Q_CHUNK
    q_c = qg.reshape(B, nc, MOBA_Q_CHUNK, kvh, G, d).transpose(1, 0, 2, 3, 4, 5)
    idx_c = idx.reshape(B, nc, MOBA_Q_CHUNK, kvh, G, kk).transpose(1, 0, 2, 3, 4, 5)
    bi = jnp.arange(B)[:, None, None, None, None]
    ki = jnp.arange(kvh)[None, None, :, None, None]

    def chunk(args):
        ci, qc, ic = args
        t0 = ci * MOBA_Q_CHUNK
        t = t0 + jnp.arange(MOBA_Q_CHUNK)
        cblk = t0 // MOBA_BLOCK
        ksel = kblk[bi, ki, ic]
        vsel = vblk[bi, ki, ic]
        s_sel = jnp.einsum('bqkgd,bqkgsnd->bqkgsn', qc, ksel).astype(jnp.float32) * scale
        slot_ok = jnp.arange(kk) < cblk
        s_sel = jnp.where(slot_ok[:, None], s_sel, NEG)
        kown = lax.dynamic_index_in_dim(kblk, cblk, axis=2, keepdims=False)
        vown = lax.dynamic_index_in_dim(vblk, cblk, axis=2, keepdims=False)
        s_own = jnp.einsum('bqkgd,bknd->bqkgn', qc, kown).astype(jnp.float32) * scale
        kpos = cblk * MOBA_BLOCK + jnp.arange(MOBA_BLOCK)
        causal = kpos[None, :] <= t[:, None]
        s_own = jnp.where(causal[None, :, None, None, :], s_own, NEG)
        nsel = kk * MOBA_BLOCK
        logits = jnp.concatenate([s_sel.reshape(B, MOBA_Q_CHUNK, kvh, G, nsel), s_own], axis=-1)
        p = jax.nn.softmax(logits, axis=-1).astype(v.dtype)
        o = jnp.einsum('bqkgm,bqkgmd->bqkgd', p[..., :nsel],
                       vsel.reshape(B, MOBA_Q_CHUNK, kvh, G, nsel, d))
        o = o + jnp.einsum('bqkgn,bknd->bqkgd', p[..., nsel:], vown)
        return o

    out = lax.map(chunk, (jnp.arange(nc), q_c, idx_c))
    return out.transpose(1, 0, 2, 3, 4, 5).reshape(B, S, H, d)

def second_inputs(seed: int = 0) -> dict:
    key = jax.random.key(seed)
    ks = jax.random.split(key, 7)
    x = jax.random.normal(ks[0], (BATCH, SEQ, D_MODEL), jnp.float32)
    norm_g = 1.0 + 0.02 * jax.random.normal(ks[1], (DEPTH_2, D_MODEL), jnp.float32)
    w_in_a = jax.random.normal(ks[2], (N_LAYERS_A, D_MODEL, IN_A), jnp.float32) * D_MODEL ** -0.5
    sinks_a = jax.random.normal(ks[3], (N_LAYERS_A, N_HEADS_2), jnp.float32)
    w_in_b = jax.random.normal(ks[4], (N_LAYERS_B, D_MODEL, IN_B), jnp.float32) * D_MODEL ** -0.5
    w_out = jax.random.normal(ks[5], (DEPTH_2, MIX_WIDTH, D_MODEL), jnp.float32) * MIX_WIDTH ** -0.5
    final_g = 1.0 + 0.02 * jax.random.normal(ks[6], (D_MODEL,), jnp.float32)
    return {"x": x, "norm_g": norm_g, "w_in_a": w_in_a, "sinks_a": sinks_a,
            "w_in_b": w_in_b, "w_out": w_out, "final_g": final_g}

def second_block(x, norm_g, w_in_a, sinks_a, w_in_b, w_out, final_g):
    B, S, _ = x.shape
    cos, sin = rope_tables(S)
    h = x
    for i in range(DEPTH_2):
        hn = rmsnorm_2(h, norm_g[i])
        j = i // N_MIXERS
        if i % N_MIXERS == 0:
            q, k, v, z = split_proj(hn, w_in_a[j], N_KV_A)
            q, k = apply_rope(q, cos, sin), apply_rope(k, cos, sin)
            o = sliding_window_sink_attention(q, k, v, sinks_a[j])
        else:
            q, k, v, z = split_proj(hn, w_in_b[j], N_KV_B)
            q, k = apply_rope(q, cos, sin), apply_rope(k, cos, sin)
            o = moba_attention(q, k, v)
        o = o.reshape(B, S, MIX_WIDTH) * jax.nn.silu(z)
        h = h + o @ w_out[i]
    return rmsnorm_2(h, final_g)


def setup_inputs(seed=0):
    out = dict(first_inputs(seed))
    for name, value in second_inputs(seed + 1).items():
        if name != "x":
            out[name + "_2"] = value
    return out


def reference(
    x, c, w_ada, b_ada, g_ffn1, w1_gate, w1_up, w1_down, g_mix, w_in, w_pool, pool_scale, w_out,
    g_ffn2, w2_gate, w2_up, w2_down, g_final, norm_g_2, w_in_a_2, sinks_a_2, w_in_b_2, w_out_2,
    final_g_2,
):
    x = first_block(
        x, c, w_ada, b_ada, g_ffn1, w1_gate, w1_up, w1_down, g_mix, w_in, w_pool, pool_scale,
        w_out, g_ffn2, w2_gate, w2_up, w2_down, g_final,
    )
    return second_block(
        x, norm_g_2, w_in_a_2, sinks_a_2, w_in_b_2, w_out_2, final_g_2,
    )


_drawn_inputs = setup_inputs


def setup_inputs(seed=0):
    import zlib

    import numpy as np

    out = dict(_drawn_inputs(seed))
    spreads = {}
    factors = {'b_ada': 2.69,
     'g_ffn1': 7.367,
     'g_mix': 4.872,
     'pool_scale': 5.284,
     'g_ffn2': 7.279,
     'norm_g_2': 8.0,
     'sinks_a_2': 5.317,
     'final_g_2': 2.943}
    for name, (base, spread) in spreads.items():
        noise = np.random.default_rng([zlib.crc32(name.encode()), seed]).standard_normal(out[name].shape)
        drawn = base * np.exp(spread * noise) if base else spread * noise
        out[name] = jnp.asarray(drawn.astype(out[name].dtype))
    for name, factor in factors.items():
        out[name] = (out[name] * factor).astype(out[name].dtype)
    return out
```

```python
from contextlib import ExitStack

import numpy as np

import concourse.bass as bass
from concourse import mybir

F32 = mybir.dt.float32
F32R = mybir.dt.float32r
ALU = mybir.AluOpType
ACT = mybir.ActivationFunctionType
AX_X = mybir.AxisListType.X

P = 128
S = 256
D = 1024
DC = D // P
F = 2816
UC = 256
UNIT = DC * UC
FB = F // UC
NS = 3
HD = 64
NEG = -1e30
EPS1, EPS2 = 1e-6, 1e-5
SCALE = HD ** -0.5
MOD_UNITS = 9 * D // UC
MOD_START = 2 * D // UC
SW = 384

C_IDENT, C_ROT, C_DIST, C_MULT, C_WIN, C_CAUSAL = 0, 128, 256, 640, 1024, 1408
C_COS, C_SIN, C_COUNT, C_END = 1792, 2048, 2304, 2368


def shape_constants():
    out = np.zeros((P, C_END), np.float32)
    out[:, C_IDENT:C_IDENT + P] = np.eye(P)
    for m in range(P):
        if m % HD < HD // 2:
            out[m + HD // 2, C_ROT + m] = -1.0
        else:
            out[m - HD // 2, C_ROT + m] = 1.0
    q = np.arange(P)[:, None]
    d = np.concatenate([q - np.arange(P)[None], P + q - np.arange(S)[None]], axis=1)
    out[:, C_DIST:C_DIST + SW] = np.maximum(d, 0)
    times = (d <= 128).astype(int) + (d % 4 == 0) + (d % 16 == 0)
    times = np.where(d >= 0, times, 0)
    out[:, C_MULT:C_MULT + SW] = np.where(times > 0, np.log(np.maximum(times, 1)), NEG)
    out[:, C_WIN:C_WIN + SW] = np.where((d >= 0) & (d < 128), 0.0, NEG)
    out[:, C_CAUSAL:C_CAUSAL + SW] = np.where(d >= 0, 0.0, NEG)
    inv = np.float32(10000.0) ** (-np.arange(0, HD, 2, dtype=np.float32) / np.float32(HD))
    ang = np.arange(S, dtype=np.float32)[None] * inv.astype(np.float32)[np.arange(P) % (HD // 2)][:, None]
    out[:, C_COS:C_COS + S] = np.cos(ang)
    out[:, C_SIN:C_SIN + S] = np.sin(ang)
    for g in range(4):
        w = 2 ** (g + 1)
        out[:, C_COUNT + 16 * g:C_COUNT + 16 * (g + 1)] = w / np.minimum(np.arange(16) + 1, w)
    return out


MIX_NORM = {"pool": 1, "window": 4, "causal": 5}


def mixer_plan():
    u, p, r, h, g, y = 3 * FB, 0, 0, 0, 0, 0
    plans = {}
    for name in ("pool", "window", "causal"):
        steps = []
        first_job, first_head, first_pair, first_y, first_rot = p, h, g, y, r
        if name == "pool":
            order = ["U0", "U1", "K0", "MAC30", "MAC31", "K1", "V0", "V1", "MOD30", "Q0", "SC0",
                     "W0", "W1", "MAC32", "MAC33", "Q1", "TPV0", "SC1",
                     "OUTA", "TPV1", "OUTB", "MOD32", "MAC34", "MAC35", "OUT1", "OUT2", "MOD34", "OUT3"]
        else:
            order = ["KV0", "Q0"] if name == "window" else ["K0", "V0", "Q0"]
            order += ["ROTK", "ROTQ", "Z0", "SC0"]
            for i in range(1, 4):
                order += [f"Q{i}", f"TPV{i - 1}", "ROTQ", f"Z{i}", f"SC{i}"]
            order += ["OUTA", "TPV3", "OUTB", "OUT1", "OUT2", "OUT3"]
        for what in order:
            kind, i = what.rstrip("0123456789"), what.lstrip("ABCDEFGHIJKLMNOPQRSTUVWXYZ")
            i = int(i) if i else 0
            st = dict(kind=kind, i=i, mixer=name)
            if kind in ("U", "K", "V", "KV", "Q", "Z", "W"):
                st.update(job=True, p=p, first=p == first_job)
                p += 1
                if kind == "W":
                    st["y"] = y
                    y += 1
                else:
                    st["u"] = u
                    u += 1
            elif kind in ("ROTK", "ROTQ"):
                st.update(r=r, p=p - 1 if kind == "ROTQ" else first_job)
                r += 1
            elif kind == "SC":
                st.update(h=h, local=h - first_head, rots=r)
                h += 4
            elif kind == "TPV":
                st.update(h=first_head + 4 * i, g=g, y=y, local=4 * i)
                g += 2
                y += 2
            elif kind in ("OUTA", "OUTB", "OUT"):
                st["u"] = u
                st["first_y"] = first_y
                if kind != "OUTA":
                    u += 1
            st["jobs"] = p
            steps.append(st)
        if name == "pool":
            u += 3 * FB
        plans[name] = steps
    assert u == 3 * FB + 12 + 3 * FB + 13 + 14
    return plans, u


PLANS, UNITS = mixer_plan()
FFN_UNIT = (0, 3 * FB + 12)
FFN_NORM = (0, 2)
RESIDUAL = {1: 0, 2: 1, 3: 2, 5: 3}


def build(nc, x, c, w_ada, b_ada, g_ffn1, w1_gate, w1_up, w1_down, g_mix, w_in, w_pool, pool_scale, w_out,
          g_ffn2, w2_gate, w2_up, w2_down, g_final, norm_g_2, w_in_a_2, sinks_a_2, w_in_b_2, w_out_2,
          final_g_2, shape_consts, out):
    with ExitStack() as ctx:
        def sb(name, shape, dt=F32):
            return ctx.enter_context(nc.sbuf_tensor(name, shape, dt))

        def sem(name):
            return ctx.enter_context(nc.semaphore(name))

        raw = sb("raw", [P, NS, UNIT])
        whi = sb("whi", [P, NS, UNIT], F32R)
        wlo = sb("wlo", [P, NS, UNIT], F32R)
        ada = sb("ada", [P, 2, DC, UC])
        macc = sb("macc", [P, 2, UC])
        hT = sb("hT", [P, DC, S])
        nhi = sb("nhi", [P, DC, S], F32R)
        nlo = sb("nlo", [P, DC, S], F32R)
        sq = sb("sq", [P, 4, S])
        tn = sb("tn", [P, 4, S])
        std = sb("std", [P, S])
        rstd = sb("rstd", [P, S])
        xo = sb("xo", [P, 2, D])
        tmp = sb("tmp", [P, 4, S + 8])
        hhi = sb("hhi", [P, 2, S], F32R)
        hlo = sb("hlo", [P, 2, S], F32R)
        pw = sb("pw", [P, 2, S + 8])
        kraw = sb("kraw", [P, 2, S])
        kd = sb("kd", [P, 4, S])
        qraw = sb("qraw", [P, 2, S])
        qT = sb("qT", [P, 2, S])
        vv = sb("vv", [P, 2, 512])
        sz = sb("sz", [P, 2, S])
        prob = sb("prob", [P, 4, SW])
        probT = sb("probT", [P, 2, SW])
        alibi = sb("alibi", [P, 2, SW])
        og = sb("og", [P, 2, S])
        yhi = sb("yhi", [P, DC, S], F32R)
        ylo = sb("ylo", [P, DC, S], F32R)
        consts = sb("consts", [P, C_END])
        ones = sb("ones", [P, P])
        zero_r = sb("zero_r", [P, 512], F32R)
        wpool = sb("wpool", [P, 4, P])
        biasT = sb("biasT", [P, 72])
        gainT = sb("gainT", [P, 60])
        cT = sb("cT", [P, DC])
        mod = sb("mod", [P, 72])
        coefA = sb("coefA", [P, 3, DC])
        gate_h = sb("gate_h", [P, 2, DC])
        sinks = sb("sinks", [P, 16])
        fgain = sb("fgain", [P, D])
        tiny = sb("tiny", [P, 4])
        mx = sb("mx", [P, 4, 2])
        nm = sb("nm", [P, 4, 2])
        den = sb("den", [P, 4, 2])
        esink = sb("esink", [P, 4, 2])
        rden = sb("rden", [P, 4, 2])
        fss = sb("fss", [P, 2, 4])
        fst = sb("fst", [P, 3, 2])
        acc = [ctx.enter_context(nc.psum_tensor(f"acc{i}", [P, 512], F32)) for i in range(4)]
        sc = [ctx.enter_context(nc.psum_tensor(f"sc{i}", [P, 512], F32)) for i in range(2)]
        tp0 = ctx.enter_context(nc.psum_tensor("tp0", [P, 512], F32))
        stat = ctx.enter_context(nc.psum_tensor("stat", [P, 512], F32))
        tp = [tp0, acc[2]]
        rot_ps = acc[2]
        o_ps = [acc[3], stat]
        ss_ps = stat[:, 0:S]
        mod0_ps, mod1_ps, mod2_ps = sc[1][:, 0:16], stat[:, S:S + 4], sc[0][:, 0:4]

        rope_c, rope_s = tn[:, 0:2], tn[:, 2:4]
        rowsA = kd[0:72, 0, 0:P]
        rowsB = kd[0:60, 1, 0:P]
        ident = consts[:, C_IDENT:C_IDENT + P]
        rotation = consts[:, C_ROT:C_ROT + P]
        cos2 = consts[:, C_COS:C_COS + S].unsqueeze(1).to_broadcast([P, 2, S])
        sin2 = consts[:, C_SIN:C_SIN + S].unsqueeze(1).to_broadcast([P, 2, S])
        cos1, sin1 = consts[:, C_COS:C_COS + S], consts[:, C_SIN:C_SIN + S]
        silu_g = tmp[:, 0:2, 0:S]
        hidden = tmp[:, 2:4, 0:S]
        c_mul = cT[:, :].unsqueeze(2).to_broadcast([P, DC, UC])

        landed = [sem(f"landed{s}") for s in range(NS)]
        hi_done = sem("hi_done")
        lo_done = sem("lo_done")
        ffn_used = sem("ffn_used")
        consts_in = sem("consts_in")
        wpool_in = sem("wpool_in")
        late_in = sem("late_in")
        rows_in = sem("rows_in")
        x_in = sem("x_in")
        ada0_in = [sem(f"ada0_in{s}") for s in range(3)]
        ada_in = [sem(f"ada_in{s}") for s in range(2)]
        set_done = sem("set_done")
        rows_t = sem("rows_t")
        gains_done = sem("gains_done")
        c_done = sem("c_done")
        x_t = sem("x_t")
        prod_done = sem("prod_done")
        macc_done = sem("macc_done")
        mod_cols = sem("mod_cols")
        mod_done = sem("mod_done")
        res_done = sem("res_done")
        sq_done = sem("sq_done")
        ss_done = sem("ss_done")
        std_done = sem("std_done")
        t_done = sem("t_done")
        nhi_done = sem("nhi_done")
        nlo_done = sem("nlo_done")
        silu_done = sem("silu_done")
        hid_done = sem("hid_done")
        hhi_done = sem("hhi_done")
        hlo_done = sem("hlo_done")
        delta = sem("delta")
        job_done = sem("job_done")
        job_out = sem("job_out")
        rot_done = sem("rot_done")
        rope_done = sem("rope_done")
        kd_done = sem("kd_done")
        pooled = sem("pooled")
        alibi_done = sem("alibi_done")
        sc_done = sem("sc_done")
        sm_read = sem("sm_read")
        nm_done = sem("nm_done")
        ex_done = sem("ex_done")
        p_done = sem("p_done")
        tp_done = sem("tp_done")
        pt_done = sem("pt_done")
        pv_done = sem("pv_done")
        og_done = sem("og_done")
        yhi_done = sem("yhi_done")
        ylo_done = sem("ylo_done")
        fin_mm = sem("fin_mm")
        fss_done = sem("fss_done")
        fstd_done = sem("fstd_done")
        fsum_done = sem("fsum_done")
        res_out = sem("res_out")
        out_sent = sem("out_sent")
        dve_step = sem("dve_step")
        act_step = sem("act_step")
        pool_step = sem("pool_step")

        block = ctx.enter_context(nc.Block())

        def rows8(t, s):
            return t[:, s, :].rearrange("p (c n) -> p c n", c=DC)

        def rows2(t, s):
            return t[:, s, :].rearrange("p (c n) -> p c n", c=2)

        def by_chunk(w):
            return w.rearrange("(c p) n -> p c n", p=P)

        w_ada_v = by_chunk(w_ada[0])
        ffn_w = [(by_chunk(w1_gate[0]), by_chunk(w1_up[0]), by_chunk(w1_down[0])),
                 (by_chunk(w2_gate[0]), by_chunk(w2_up[0]), by_chunk(w2_down[0]))]
        in_w = {"pool": by_chunk(w_in[0]), "window": by_chunk(w_in_a_2[0]), "causal": by_chunk(w_in_b_2[0])}
        out_w = {"pool": by_chunk(w_out[0]), "window": by_chunk(w_out_2[0]), "causal": by_chunk(w_out_2[1])}
        first_col = {"pool": dict(U=0, Q=512, K=1024, V=1536), "window": dict(Q=0, KV=1024, Z=1280),
                     "causal": dict(Q=0, K=1024, V=1280, Z=1536)}
        gain_col = {0: 0, 1: 8, 2: 16, 3: 24, 4: 32, 5: 40}

        def norm_gain(k, m):
            return coefA[:, k, m:m + 1] if k < 3 else gainT[:, gain_col[k] + m:gain_col[k] + m + 1]

        def norm_shift(k, m):
            return mod[:, 24 * k + m:24 * k + m + 1] if k < 3 else tiny[:, 2:3]

        def head_place(mixer, local):
            kv = {"pool": local // 2, "window": local // 8, "causal": local // 4}[mixer]
            v = {"pool": local, "window": local // 8, "causal": local // 4}[mixer]
            return local % 2, kv, HD * v

        @block.sync
        def _(sp):
            def load_unit(u, view, add=0, reps=None):
                if u >= NS or reps is not None:
                    sp.wait_ge(lo_done, u - NS + 1 + (3 * reps if reps is not None else 0))
                sp.dma_start(raw[:, u % NS, :].rearrange("p (c n) -> p c n", c=view.shape[1]),
                             view).then_inc(landed[u % NS], 16)

            def load_ada(a, col, reps=None):
                sp.wait_ge(macc_done, a - 1 + (2 * reps if reps is not None else 0))
                sp.dma_start(ada[:, a % 2], w_ada_v[:, :, bass.ds(col, UC)]).then_inc(ada_in[a % 2], 16)

            sp.dma_start(rowsB[52:60, :], c.rearrange("a (k p) -> (a k) p", p=P)).then_inc(rows_in, 16)
            for at, g in ((0, g_ffn1), (8, g_mix), (16, g_ffn2), (32, norm_g_2), (48, pool_scale)):
                rows = g.rearrange("a (k p) -> (a k) p", p=P)
                sp.dma_start(rowsB[at:at + rows.shape[0], :], rows).then_inc(rows_in, 16)
            sp.dma_start(rowsB[24:32, :], g_final.rearrange("(k p) -> k p", p=P)).then_inc(rows_in, 16)
            sp.dma_start(rowsA, b_ada.rearrange("a (k p) -> (a k) p", p=P)).then_inc(rows_in, 16)
            sp.dma_start(consts[:, :], shape_consts).then_inc(consts_in, 16)
            for a in range(MOD_START):
                if a >= 3:
                    sp.wait_ge(macc_done, a - 2)
                to = ada[:, a % 3] if a % 3 < 2 else rows8(raw, 2)
                sp.dma_start(to, w_ada_v[:, :, a * UC:(a + 1) * UC]).then_inc(ada0_in[a % 3], 16)
                if a == 2:
                    sp.dma_start(xo[:, :, :], x[0].rearrange("(b p) n -> p b n", p=P)).then_inc(x_in, 16)
                if a == 5:
                    load_unit(0, ffn_w[0][0][:, :, 0:UC])
                if a == 6:
                    load_unit(1, ffn_w[0][1][:, :, 0:UC])
            sp.wait_ge(macc_done, 6)
            for f in range(2):
                base = FFN_UNIT[f]
                gate, up, down = ffn_w[f]
                if f == 1:
                    load_unit(base, gate[:, :, 0:UC])
                    load_unit(base + 1, up[:, :, 0:UC])
                first = f == 0
                if first:
                    sp.dma_start(rows8(raw, 2), gate[:, :, UC:2 * UC]).then_inc(landed[2], 16)
                    load_unit(3, up[:, :, UC:2 * UC])
                    load_unit(4, down[:, 0:2, :])
                    load_ada(8, 8 * UC)
                    load_ada(9, 9 * UC)
                with sp.Fori(1 if first else 0, FB - 1) as j:
                    u = base + 2
                    load_unit(u, gate[:, :, bass.ds(j * UC + UC, UC)], reps=j)
                    load_unit(u + 1, up[:, :, bass.ds(j * UC + UC, UC)], reps=j)
                    load_unit(u + 2, down[:, bass.ds(j * 2, 2), :], reps=j)
                    if first:
                        load_ada(8, j * 2 * UC + 8 * UC, reps=j)
                        load_ada(9, j * 2 * UC + 9 * UC, reps=j)
                load_unit(base + 32, down[:, 2 * (FB - 1):2 * FB, :])
                if first:
                    load_ada(28, 28 * UC)
                    load_ada(29, 29 * UC)
                    sp.dma_start(wpool[:, :, :], w_pool[0].rearrange("g c d -> c g d")).then_inc(wpool_in, 16)
                    ada_after = {3 * FB + 2: (30, 31), 3 * FB + 5: (32, 33), 3 * FB + 10: (34, 35)}
                for name in ("pool",) if first else ("window", "causal"):
                    for st in PLANS[name]:
                        if "u" not in st or st["kind"] == "OUTA":
                            continue
                        n = st["i"] if st["kind"] != "OUTB" else 0
                        if st["kind"] in ("OUTB", "OUT"):
                            load_unit(st["u"], out_w[name][:, :, n * UC:(n + 1) * UC])
                        else:
                            at = first_col[name][st["kind"]] + n * UC
                            load_unit(st["u"], in_w[name][:, :, at:at + UC])
                        for a in ada_after.get(st["u"], ()):
                            load_ada(a, a * UC)
                if first:
                    sp.dma_start(fgain[:, :], final_g_2.rearrange("(a n) -> a n", a=1).to_broadcast([P, D])
                                 ).then_inc(late_in, 16)
                    sp.dma_start(sinks[:, :], sinks_a_2.to_broadcast([P, 16])).then_inc(late_in, 16)
            for j in range(4):
                sp.wait_ge(res_out, j + 1)
                sp.dma_start(out[0].rearrange("(b p) n -> p b n", p=P)[:, :, j * UC:(j + 1) * UC],
                             xo[:, :, j * UC:(j + 1) * UC]).then_inc(out_sent, 16)
            sp.wait_ge(out_sent, 64)

        @block.gpsimd
        def _(pool):
            steps = [0]

            def link(ins):
                steps[0] += 1
                ins.then_inc(pool_step, 1)
                pool.wait_ge(pool_step, steps[0])

            def product(a, reps=None):
                n = 16 * ((a - MOD_START) // 2 + 1)
                pool.wait_ge(ada_in[a % 2], n + 16 * reps if reps is not None else n)
                nc.gpsimd.tensor_tensor(ada[:, a % 2], ada[:, a % 2], c_mul, ALU.mult).then_inc(prod_done, 1)

            nc.gpsimd.memset(ones[:, :], 1.0).then_inc(set_done, 1)
            nc.gpsimd.memset(zero_r[:, :].bitcast(F32), 0.0).then_inc(set_done, 1)
            nc.gpsimd.memset(pw[:, :, :], 0.0).then_inc(set_done, 1)
            pool.wait_ge(c_done, 1)
            product(8)
            product(9)
            with pool.Fori(0, FB - 1) as j:
                product(10, reps=j)
                product(11, reps=j)

            def bias(h):
                if h >= 2:
                    pool.wait_ge(sm_read, h - 1)
                slope = 2.0 ** (-8.0 * (h + 1) / 8)
                link(nc.gpsimd.tensor_scalar(alibi[:, h % 2], consts[:, C_DIST:C_DIST + SW], -slope, None, ALU.mult))
                nc.gpsimd.tensor_tensor(alibi[:, h % 2], alibi[:, h % 2], consts[:, C_MULT:C_MULT + SW],
                                        ALU.add).then_inc(alibi_done, 1)

            def pooling(g):
                src = tmp[:, g]
                own = tmp[:, g, 8:8 + S]
                for i in range(g + 1):
                    to = pw[:, i % 2]
                    link(nc.gpsimd.tensor_tensor(to[:, 8:8 + S], src[:, 8:8 + S], src[:, 8 - 2 ** i:8 - 2 ** i + S],
                                                 ALU.add))
                    src = to
                win = src[:, 8:8 + S]
                link(nc.gpsimd.tensor_scalar(win, win, 1.0 / 2 ** (g + 1), None, ALU.mult))
                link(nc.gpsimd.tensor_tensor(win[:, 0:16], win[:, 0:16],
                                             consts[:, C_COUNT + 16 * g:C_COUNT + 16 * (g + 1)], ALU.mult))
                ins = nc.gpsimd.tensor_tensor(own, win, own, ALU.subtract)
                ins.then_inc(pooled, 1)
                pool.wait_ge(pooled, g + 1)

            pool.wait_ge(consts_in, 16)
            bias(0)
            bias(1)
            pool.wait_ge(hlo_done, FB)
            link(nc.gpsimd.memset(tmp[:, :, 0:8], 0.0))
            for st in PLANS["pool"]:
                if st["kind"] == "U":
                    pool.wait_ge(job_out, st["p"] + 1)
                    pooling(2 * st["i"])
                    pooling(2 * st["i"] + 1)
                elif st["kind"] == "SC":
                    for h in range(max(2, 4 * st["i"]), 4 * st["i"] + 4):
                        bias(h)
                elif st["kind"] == "MAC":
                    product(st["i"])

        @block.scalar
        def _(act):
            def high(u, reps=None, by=None):
                if u >= UNITS:
                    return
                n = 16 * (u // NS + 1)
                act.wait_ge(landed[u % NS], n + 16 * reps if reps is not None else n)
                nc.scalar.activation(whi[:, u % NS], raw[:, u % NS], ACT.Copy).then_inc(hi_done, 1)

            def squares(k, chunks=range(DC)):
                for m in chunks:
                    act.wait_ge(res_done, DC * k + m + 1)
                    if m >= 4:
                        act.wait_ge(ss_done, DC * k + m - 3)
                    nc.scalar.activation(sq[:, m % 4], hT[:, m], ACT.Square).then_inc(sq_done, 1)

            def deviation(k):
                act.wait_ge(ss_done, DC * (k + 1))
                eps = tiny[:, 0:1] if k <= 3 else tiny[:, 1:2]
                nc.scalar.activation(std[:, :], ss_ps, ACT.Sqrt, bias=eps, scale=1.0 / D).then_inc(std_done, 1)

            def norm_high(k):
                for m in range(DC):
                    act.wait_ge(t_done, DC * tnum[k] + m + 1)
                    nc.scalar.activation(nhi[:, m], tn[:, m % 4], ACT.Identity,
                                         bias=norm_shift(k, m)).then_inc(nhi_done, 1)

            def job(st):
                act.wait_ge(job_done, st["p"] + 1)
                bank = acc[st["p"] % 2]
                pair = bank[:, :].rearrange("p (b n) -> p b n", b=2)
                kind, i, mixer = st["kind"], st["i"], st["mixer"]
                if kind == "U":
                    ins = nc.scalar.activation(tmp[:, 2 * i:2 * i + 2, 8:8 + S], pair, ACT.Copy)
                elif kind == "K":
                    to = kd[:, 2 * i:2 * i + 2] if mixer == "pool" else kraw[:, :, :]
                    ins = nc.scalar.activation(to, pair, ACT.Copy)
                elif kind == "V":
                    ins = nc.scalar.activation(vv[:, :, UC * i:UC * (i + 1)], pair, ACT.Copy)
                elif kind == "KV":
                    nc.scalar.activation(kraw[:, 0], bank[:, 0:S], ACT.Copy)
                    ins = nc.scalar.activation(vv[:, :, 0:P], bank[:, S:2 * S].rearrange("p (b n) -> p b n", b=2),
                                               ACT.Copy)
                elif kind == "Q":
                    ins = nc.scalar.activation(qT[:, :, :] if mixer == "pool" else qraw[:, :, :], pair, ACT.Copy,
                                               scale=SCALE)
                elif kind == "Z":
                    if i:
                        act.wait_ge(og_done, z_pairs[mixer] + 2 * i)
                    ins = nc.scalar.activation(sz[:, :, :], pair, ACT.Silu)
                else:
                    if i:
                        act.wait_ge(ylo_done, st["y"])
                    for n in range(2):
                        ch = 48 + 2 * i + n
                        ins = nc.scalar.activation(kraw[:, n], pair[:, n], ACT.Copy, scale=gainT[:, ch:ch + 1])
                ins.then_inc(job_out, 1)
                if kind == "W":
                    act.wait_ge(job_out, st["p"] + 1)
                    nc.scalar.activation(yhi[:, 2 * i:2 * i + 2], kraw[:, :, :], ACT.Copy).then_inc(yhi_done, 1)
                else:
                    high(st["u"] + NS)

            def duplicate(st):
                act.wait_ge(rope_done, st["r"] + 1)
                for half in range(2):
                    for src in range(2):
                        if st["mixer"] == "window":
                            to, of = kd[64 * half:64 * half + 64, src], kraw[64 * src:64 * src + 64, 0]
                        else:
                            to, of = kd[64 * half:64 * half + 64, src::2], kraw[64 * src:64 * src + 64, :]
                        ins = nc.scalar.activation(to, of, ACT.Copy)
                ins.then_inc(kd_done, 1)

            def softmax(st):
                for n in range(4):
                    h = st["h"] + n
                    s = h % 4
                    act.wait_ge(nm_done, h + 1)
                    if st["mixer"] == "window":
                        head = st["local"] + n
                        nc.scalar.activation(esink[:, s], nm[:, s], ACT.Exp, bias=sinks[:, head:head + 1])
                    for b, (lo, up) in enumerate(((0, P), (P, SW))):
                        ins = nc.scalar.activation(prob[:, s, lo:up], prob[:, s, lo:up], ACT.Exp,
                                                   bias=nm[:, s, b:b + 1], accum_out=den[:, s, b:b + 1])
                    ins.then_inc(ex_done, 1)

            def outputs(st):
                for n in range(4):
                    h = st["h"] + n
                    act.wait_ge(tp_done, h + 1)
                    nc.scalar.activation(probT[:, h % 2], tp[h % 2][:, 0:SW], ACT.Copy).then_inc(pt_done, 1)
                    if n >= 2:
                        g = st["g"] + n - 2
                        act.wait_ge(og_done, g + 1)
                        nc.scalar.activation(yhi[:, y_chunk(st, n - 2)], og[:, g % 2], ACT.Copy).then_inc(yhi_done, 1)

            def mixer(name):
                for st in PLANS[name]:
                    if st.get("job"):
                        job(st)
                    elif st["kind"] == "ROTK":
                        duplicate(st)
                    elif st["kind"] == "SC":
                        softmax(st)
                    elif st["kind"] == "TPV":
                        outputs(st)
                    elif st["kind"] in ("OUTB", "OUT"):
                        j = st["i"]
                        if name == "causal":
                            act.wait_ge(fin_mm, j + 1)
                        else:
                            k = MIX_NORM[name] + 1
                            act.wait_ge(delta, DC * RESIDUAL[k] + 2 * j + 2)
                            squares(k, range(2 * j, 2 * j + 2))
                        high(st["u"] + NS)

            def ffn(f):
                base, n0 = FFN_UNIT[f], FB * f
                done = (FB * 3 - 1) * f

                def silu(i, reps=None):
                    add = reps if reps is not None else 0
                    if n0 + i > 0:
                        act.wait_ge(hid_done, n0 + i + add)
                    nc.scalar.activation(silu_g, sc[0][:, :].rearrange("p (b n) -> p b n", b=2),
                                         ACT.Silu).then_inc(silu_done, 1)

                def hidden_high(i, reps=None):
                    act.wait_ge(hid_done, n0 + i + 1 + (reps if reps is not None else 0))
                    nc.scalar.activation(hhi[:, :, :], hidden, ACT.Copy).then_inc(hhi_done, 1)

                act.wait_ge(ffn_used, done + 1)
                silu(0)
                high(base + 3)
                act.wait_ge(ffn_used, done + 2)
                high(base + 4)
                hidden_high(0)
                with act.Fori(0, FB - 1) as j:
                    u = base + 2
                    act.wait_ge(ffn_used, 3 * j + (done + 3))
                    silu(1, reps=j)
                    high(u + 3, reps=j)
                    act.wait_ge(ffn_used, 3 * j + (done + 4))
                    high(u + 4, reps=j)
                    act.wait_ge(ffn_used, 3 * j + (done + 5))
                    hidden_high(1, reps=j)
                    high(u + 5, reps=j)
                squares(FFN_NORM[f] + 1)
                high(base + 3 * FB + 2)

            act.wait_ge(gains_done, 2)
            nc.scalar.activation(cT[:, :], gainT[:, 52:60], ACT.Silu).then_inc(c_done, 1)
            act.wait_ge(set_done, 4)
            squares(0)
            deviation(0)
            high(0)
            norm_high(0)
            high(1)
            high(2)
            ffn(0)
            deviation(1)
            norm_high(1)
            mixer("pool")
            deviation(2)
            norm_high(2)
            ffn(1)
            deviation(3)
            squares(4)
            deviation(4)
            norm_high(4)
            act.wait_ge(late_in, 32)
            mixer("window")
            deviation(5)
            norm_high(5)
            mixer("causal")
            for j in range(4):
                act.wait_ge(fin_mm, j + 1)
                for b in range(2):
                    ins = nc.scalar.activation((sq, tn)[j // 2][:, 2 * (j % 2) + b], acc[j][:, b * S:(b + 1) * S], ACT.Square,
                                               accum_out=fss[:, b, j:j + 1])
                ins.then_inc(fss_done, 1)
            act.wait_ge(fsum_done, 1)
            nc.scalar.activation(fst[:, 1], fst[:, 0], ACT.Sqrt, bias=tiny[:, 1:2], scale=1.0 / D).then_inc(fstd_done, 1)

        @block.vector
        def _(dve):
            steps = [0]

            def link(ins):
                steps[0] += 1
                ins.then_inc(dve_step, 1)
                dve.wait_ge(dve_step, steps[0])

            def low(u, reps=None):
                if u >= UNITS:
                    return
                dve.wait_ge(hi_done, u + 1 + (3 * reps if reps is not None else 0))
                nc.vector.tensor_tensor(wlo[:, u % NS], raw[:, u % NS], whi[:, u % NS].bitcast(F32),
                                        ALU.subtract).then_inc(lo_done, 1)

            def residual(k, chunks=range(DC)):
                for m in chunks:
                    dve.wait_ge(delta, DC * RESIDUAL[k] + 2 * (m // 2) + 2)
                    bank = acc[m // 2] if k in (1, 3) else acc[(m // 2) % 2]
                    upd = bank[:, (m % 2) * S:(m % 2 + 1) * S]
                    if k == 5:
                        ins = nc.vector.tensor_tensor(hT[:, m], upd, hT[:, m], ALU.add)
                    else:
                        gate = mod[:, 40 + m:41 + m] if k == 2 else gate_h[:, k // 2, m:m + 1]
                        ins = nc.vector.scalar_tensor_tensor(out=hT[:, m], in0=upd, scalar=gate, in1=hT[:, m],
                                                             op0=ALU.mult, op1=ALU.add)
                    ins.then_inc(res_done, 1)

            def normalise(k):
                dve.wait_ge(std_done, k + 1)
                link(nc.vector.reciprocal(rstd[:, :], std[:, :]))
                for m in range(DC + 1):
                    if m < DC:
                        if k == 3:
                            nc.vector.scalar_tensor_tensor(out=hT[:, m], in0=hT[:, m], scalar=norm_gain(k, m),
                                                           in1=rstd[:, :], op0=ALU.mult,
                                                           op1=ALU.mult).then_inc(res_done, 1)
                            continue
                        if m >= 4:
                            dve.wait_ge(nlo_done, DC * tnum[k] + m - 3)
                        nc.vector.scalar_tensor_tensor(out=tn[:, m % 4], in0=hT[:, m], scalar=norm_gain(k, m),
                                                       in1=rstd[:, :], op0=ALU.mult, op1=ALU.mult).then_inc(t_done, 1)
                    if m > 0 and k != 3:
                        n = m - 1
                        dve.wait_ge(nhi_done, DC * tnum[k] + n + 1)
                        nc.vector.scalar_tensor_tensor(out=nlo[:, n], in0=tn[:, n % 4], scalar=norm_shift(k, n),
                                                       in1=nhi[:, n].bitcast(F32), op0=ALU.add,
                                                       op1=ALU.subtract).then_inc(nlo_done, 1)

            def reduce_products(a, reps=None):
                n = a - MOD_START + 1
                dve.wait_ge(prod_done, n + (2 * reps if reps is not None else 0))
                dve.wait_ge(mod_cols, a - 1 + (2 * reps if reps is not None else 0))
                nc.vector.tensor_reduce(macc[:, a % 2], ada[:, a % 2].rearrange("p c n -> p n c"), AX_X,
                                        ALU.add).then_inc(macc_done, 1)

            def mod_out(a, count=2, reps=None):
                n = 2 * count
                add = 2 * reps if reps is not None else 0
                dve.wait_ge(mod_cols, a + count + add)
                ps = mod0_ps if a == 0 else mod1_ps if a < 30 else mod2_ps
                at = 2 * a if reps is None else reps * 4 + 2 * a
                nc.vector.tensor_tensor(mod[:, bass.ds(at, n)], ps, biasT[:, bass.ds(at, n)],
                                        ALU.add).then_inc(mod_done, count)

            def coefficient(k):
                return nc.vector.scalar_tensor_tensor(
                    out=coefA[:, k], in0=mod[:, 24 * k + 8:24 * k + 16], scalar=1.0,
                    in1=gainT[:, gain_col[k]:gain_col[k] + 8], op0=ALU.add, op1=ALU.mult)

            def job(st):
                if st["kind"] == "W":
                    dve.wait_ge(yhi_done, st["y"] + 1)
                    i = st["i"]
                    nc.vector.tensor_tensor(ylo[:, 2 * i:2 * i + 2], kraw[:, :, :], yhi[:, 2 * i:2 * i + 2].bitcast(F32),
                                            ALU.subtract).then_inc(ylo_done, 1)
                else:
                    low(st["u"] + NS)

            def rope(st):
                one = st["mixer"] == "window" and st["kind"] == "ROTK"
                dve.wait_ge(job_out, st["p"] + 1)
                if st["r"]:
                    dve.wait_ge(rope_done, st["r"])
                if one:
                    src, ps = kraw[:, 0], rot_ps[:, 0:S]
                    a, b, to, co, si = rope_c[:, 0], rope_s[:, 0], kraw[:, 0], cos1, sin1
                else:
                    src = kraw[:, :, :] if st["kind"] == "ROTK" else qraw[:, :, :]
                    ps = rot_ps[:, :].rearrange("p (b n) -> p b n", b=2)
                    a, b, co, si = rope_c, rope_s, cos2, sin2
                    to = kraw[:, :, :] if st["kind"] == "ROTK" else qT[:, :, :]
                nc.vector.tensor_tensor(a, src, co, ALU.mult).then_inc(dve_step, 1)
                dve.wait_ge(rot_done, st["r"] + 1)
                steps[0] += 1
                link(nc.vector.tensor_tensor(b, ps, si, ALU.mult))
                nc.vector.tensor_tensor(to, a, b, ALU.add).then_inc(rope_done, 1)

            def masked_max(st, n):
                h = st["h"] + n
                s = h % 4
                dve.wait_ge(sc_done, h + 1)
                if st["mixer"] == "pool":
                    dve.wait_ge(alibi_done, h + 1)
                    mask = alibi[:, h % 2]
                else:
                    at = C_WIN if st["mixer"] == "window" else C_CAUSAL
                    mask = consts[:, at:at + SW]
                for b, (lo, up) in enumerate(((0, P), (P, SW))):
                    ins = nc.vector.tensor_tensor_reduce(out=prob[:, s, lo:up], in0=sc[h % 2][:, lo:up],
                                                         in1=mask[:, lo:up], scale=1.0, scalar=NEG,
                                                         op0=ALU.add, op1=ALU.max, accum_out=mx[:, s, b:b + 1])
                ins.then_inc(sm_read, 1)
                dve.wait_ge(sm_read, h + 1)
                if st["mixer"] == "window":
                    head = st["local"] + n
                    nc.vector.tensor_scalar(nm[:, s], mx[:, s], sinks[:, head:head + 1], -1.0, ALU.max,
                                            ALU.mult).then_inc(nm_done, 1)
                else:
                    nc.vector.tensor_scalar(nm[:, s], mx[:, s], -1.0, None, ALU.mult).then_inc(nm_done, 1)

            def divide(st, n):
                h = st["h"] + n
                s = h % 4
                dve.wait_ge(ex_done, h + 1)
                if st["mixer"] == "window":
                    link(nc.vector.tensor_tensor(den[:, s], den[:, s], esink[:, s], ALU.add))
                link(nc.vector.reciprocal(rden[:, s], den[:, s]))
                for b, (lo, up) in enumerate(((0, P), (P, SW))):
                    ins = nc.vector.tensor_scalar(prob[:, s, lo:up], prob[:, s, lo:up], rden[:, s, b:b + 1], None,
                                                  ALU.mult)
                ins.then_inc(p_done, 1)

            def outputs(st):
                for n in range(2):
                    g = st["g"] + n
                    dve.wait_ge(pv_done, g + 1)
                    dve.wait_ge(ylo_done, st["y"] + n - 1)
                    o = o_ps[n][:, 0:S]
                    if st["mixer"] == "pool":
                        ins = nc.vector.tensor_copy(og[:, g % 2], o)
                    else:
                        ins = nc.vector.tensor_tensor(og[:, g % 2], o, sz[:, n], ALU.mult)
                    ins.then_inc(og_done, 1)
                    ch = y_chunk(st, n)
                    dve.wait_ge(yhi_done, st["y"] + n + 1)
                    nc.vector.tensor_tensor(ylo[:, ch], og[:, g % 2], yhi[:, ch].bitcast(F32),
                                            ALU.subtract).then_inc(ylo_done, 1)

            def mixer(name):
                for st in PLANS[name]:
                    kind = st["kind"]
                    if st.get("job"):
                        job(st)
                    elif kind in ("ROTK", "ROTQ"):
                        rope(st)
                    elif kind == "SC":
                        for n in range(4):
                            masked_max(st, n)
                            if n:
                                divide(st, n - 1)
                        divide(st, 3)
                    elif kind == "TPV":
                        outputs(st)
                    elif kind in ("OUTB", "OUT"):
                        if name != "causal":
                            residual(MIX_NORM[name] + 1, range(2 * st["i"], 2 * st["i"] + 2))
                        low(st["u"] + NS)
                    elif kind == "MAC":
                        reduce_products(st["i"])
                    elif kind == "MOD":
                        mod_out(st["i"])

            def ffn(f):
                base, n0 = FFN_UNIT[f], FB * f
                done = (FB * 3 - 1) * f
                up_ps = sc[1][:, :].rearrange("p (b n) -> p b n", b=2)

                def hidden_product(i, reps=None):
                    add = reps if reps is not None else 0
                    dve.wait_ge(silu_done, n0 + i + 1 + add)
                    if n0 + i > 0:
                        dve.wait_ge(hlo_done, n0 + i + add)
                    nc.vector.tensor_tensor(hidden, silu_g, up_ps, ALU.mult).then_inc(hid_done, 1)

                def hidden_low(i, reps=None):
                    dve.wait_ge(hhi_done, n0 + i + 1 + (reps if reps is not None else 0))
                    nc.vector.tensor_tensor(hlo[:, :, :], hidden, hhi[:, :, :].bitcast(F32),
                                            ALU.subtract).then_inc(hlo_done, 1)

                low(base + 3)
                dve.wait_ge(ffn_used, done + 2)
                hidden_product(0)
                low(base + 4)
                hidden_low(0)
                if f == 0:
                    reduce_products(8)
                    reduce_products(9)
                with dve.Fori(0, FB - 1) as j:
                    u = base + 2
                    low(u + 3, reps=j)
                    dve.wait_ge(ffn_used, 3 * j + (done + 4))
                    hidden_product(1, reps=j)
                    low(u + 4, reps=j)
                    hidden_low(1, reps=j)
                    low(u + 5, reps=j)
                    if f == 0:
                        mod_out(8, reps=j)
                        reduce_products(10, reps=j)
                        reduce_products(11, reps=j)
                if f == 0:
                    mod_out(28)
                    dve.wait_ge(mod_done, 30)
                    nc.vector.tensor_scalar(gate_h[:, 0], mod[:, 16:24], 0.5, None, ALU.mult)
                    link(coefficient(1))
                residual(FFN_NORM[f] + 1)
                low(base + 3 * FB + 2)

            nc.vector.memset(tiny[:, 0:1], EPS1)
            nc.vector.memset(tiny[:, 1:2], EPS2)
            nc.vector.memset(tiny[:, 2:3], 0.0).then_inc(set_done, 1)
            dve.wait_ge(rows_t, 2)
            nc.vector.tensor_copy(biasT[:, :], sc[0][:, 0:72]).then_inc(gains_done, 1)
            nc.vector.tensor_copy(gainT[:, :], sc[0][:, 128:188]).then_inc(gains_done, 1)
            dve.wait_ge(c_done, 1)

            def start_unit(a):
                dve.wait_ge(ada0_in[a % 3], 16 * (a // 3 + 1))
                if a >= 2:
                    dve.wait_ge(mod_cols, a - 1)
                src = ada[:, a % 3] if a % 3 < 2 else rows8(raw, 2)
                link(nc.vector.tensor_scalar(macc[:, a % 2], src[:, 0], cT[:, 0:1], None, ALU.mult))
                for k in range(1, DC):
                    ins = nc.vector.scalar_tensor_tensor(out=macc[:, a % 2], in0=src[:, k], scalar=cT[:, k:k + 1],
                                                         in1=macc[:, a % 2], op0=ALU.mult, op1=ALU.add)
                    if k < DC - 1:
                        link(ins)
                    else:
                        ins.then_inc(macc_done, 1)

            for a in range(MOD_START):
                start_unit(a)
                if a == 3:
                    for m in range(DC):
                        dve.wait_ge(x_t, 2 * (m // 2) + 2)
                        nc.vector.tensor_copy(hT[:, m], acc[m // 2][:, (m % 2) * S:(m % 2 + 1) * S]
                                              ).then_inc(res_done, 1)
                if a == 6:
                    low(0)
            mod_out(0, MOD_START)
            dve.wait_ge(mod_done, MOD_START)
            link(coefficient(0))
            normalise(0)
            low(1)
            low(2)
            ffn(0)
            normalise(1)
            mixer("pool")
            dve.wait_ge(mod_done, MOD_UNITS)
            nc.vector.tensor_scalar(gate_h[:, 1], mod[:, 64:72], 0.5, None, ALU.mult)
            link(coefficient(2))
            normalise(2)
            ffn(1)
            normalise(3)
            normalise(4)
            dve.wait_ge(late_in, 32)
            mixer("window")
            normalise(5)
            mixer("causal")
            dve.wait_ge(fss_done, 4)
            nc.vector.tensor_reduce(fst[:, 0], fss[:, :, :], AX_X, ALU.add).then_inc(fsum_done, 1)
            dve.wait_ge(fstd_done, 1)
            link(nc.vector.reciprocal(fst[:, 2], fst[:, 1]))
            for j in range(4):
                for b in range(2):
                    ins = nc.vector.scalar_tensor_tensor(
                        out=xo[:, b, j * UC:(j + 1) * UC], in0=acc[j][:, b * S:(b + 1) * S],
                        scalar=fst[:, 2, b:b + 1], in1=fgain[:, j * UC:(j + 1) * UC], op0=ALU.mult, op1=ALU.mult)
                ins.then_inc(res_out, 1)

        @block.tensor
        def _(pe):
            mm = nc.tensor.matmul

            def split_product(to, stat_hi, stat_lo, mov_hi, mov_lo, first, last):
                mm(to, stat_hi, mov_hi, start=first, stop=False, skip_group_check=True)
                mm(to, stat_hi, mov_lo, start=False, stop=False, skip_group_check=True)
                return mm(to, stat_lo, mov_hi, start=False, stop=last, skip_group_check=True)

            def sum_squares(k, m):
                pe.wait_ge(sq_done, DC * k + m + 1)
                mm(ss_ps, ones[:, :], sq[:, m % 4], start=(m == 0), stop=(m == DC - 1)).then_inc(ss_done, 1)

            def mod_sum(a, to, reps=None):
                pe.wait_ge(macc_done, a + 1 + (2 * reps if reps is not None else 0))
                for n in range(2):
                    ins = mm(to[:, n:n + 1], macc[:, a % 2, n * P:(n + 1) * P], ones[:, 0:1],
                             start=True, stop=True)
                ins.then_inc(mod_cols, 1)

            def project(bank, slot, k=None, cols=2):
                hi, lo = rows8(whi, slot), rows8(wlo, slot)
                for m in range(cols):
                    for ch in range(DC):
                        if k is not None and m == 0:
                            pe.wait_ge(nlo_done, DC * tnum[k] + ch + 1)
                        at = slice(m * P, (m + 1) * P)
                        ins = split_product(bank[:, m * S:(m + 1) * S], hi[:, ch, at], lo[:, ch, at],
                                            nhi[:, ch], nlo[:, ch], ch == 0, ch == DC - 1)
                return ins

            def project_rows(bank, slot, col, width, at0):
                hi, lo = rows8(whi, slot), rows8(wlo, slot)
                for b in range(2):
                    for ch in range(DC):
                        tok = slice(b * P, (b + 1) * P)
                        to = bank[:, at0 + b * width:at0 + (b + 1) * width]
                        w = slice(col, col + width)
                        mm(to, nhi[:, ch, tok], hi[:, ch, w], start=(ch == 0), stop=False, skip_group_check=True)
                        mm(to, nhi[:, ch, tok], lo[:, ch, w], start=False, stop=False, skip_group_check=True)
                        ins = mm(to, nlo[:, ch, tok], hi[:, ch, w], start=False, stop=(ch == DC - 1),
                                 skip_group_check=True)
                return ins

            def job(st):
                kind, p = st["kind"], st["p"]
                if p >= 2:
                    pe.wait_ge(job_out, p - 1)
                bank = acc[p % 2]
                if kind == "W":
                    pe.wait_ge(pooled, 2 * st["i"] + 2)
                    pe.wait_ge(wpool_in, 16)
                    for n in range(2):
                        g = 2 * st["i"] + n
                        ins = mm(bank[:, n * S:(n + 1) * S], wpool[:, g], tmp[:, g, 8:8 + S], start=True, stop=True)
                    ins.then_inc(job_done, 1)
                    return
                u = st["u"]
                pe.wait_ge(lo_done, u + 1)
                k = MIX_NORM[st["mixer"]] if st["first"] else None
                if kind == "V":
                    ins = project_rows(bank, u % NS, 0, UC, 0)
                elif kind == "KV":
                    project(bank, u % NS, k, cols=1)
                    ins = project_rows(bank, u % NS, P, P, S)
                else:
                    ins = project(bank, u % NS, k)
                ins.then_inc(job_done, 1)

            def rotate(st):
                pe.wait_ge(job_out, st["p"] + 1)
                if st["r"]:
                    pe.wait_ge(rope_done, st["r"])
                if st["h_before"]:
                    pe.wait_ge(pt_done, st["h_before"])
                if st["kind"] == "ROTK" and st["mixer"] == "window":
                    mm(rot_ps[:, 0:S], rotation, kraw[:, 0], start=True, stop=True).then_inc(rot_done, 1)
                else:
                    src = kraw if st["kind"] == "ROTK" else qraw
                    mm(rot_ps[:, :], rotation, src[:, :, :].rearrange("p b n -> p (b n)"), start=True,
                       stop=True).then_inc(rot_done, 1)

            def scores(st):
                if st["mixer"] == "pool":
                    pe.wait_ge(job_out, st["jobs"])
                    pe.wait_ge(mod_done, 32)
                else:
                    pe.wait_ge(rope_done, st["rots"])
                    pe.wait_ge(kd_done, 1 if st["mixer"] == "window" else 2)
                for n in range(4):
                    h = st["h"] + n
                    half, kv, _ = head_place(st["mixer"], st["local"] + n)
                    if h >= 2:
                        pe.wait_ge(sm_read, h - 1)
                    part = slice(64 * half, 64 * half + 64)
                    mm(sc[h % 2][:, 0:P], qT[part, n // 2, 0:P], kd[part, kv, 0:P], start=True, stop=True)
                    mm(sc[h % 2][:, P:SW], qT[part, n // 2, P:S], kd[part, kv, :], start=True,
                       stop=True).then_inc(sc_done, 1)

            def transposes(st, n):
                h = st["h"] + n
                pe.wait_ge(p_done, h + 1)
                if h >= 2:
                    pe.wait_ge(pt_done, h - 1)
                for i in range(3):
                    ins = nc.tensor.transpose(tp[h % 2][:, i * P:(i + 1) * P], prob[:, h % 4, i * P:(i + 1) * P], ident)
                ins.then_inc(tp_done, 1)

            def values(st, n):
                h, g = st["h"] + n, st["g"] + n // 2
                half, _, col = head_place(st["mixer"], st["local"] + n)
                pe.wait_ge(pt_done, h + 1)
                if n % 2 == 0 and g >= 2:
                    pe.wait_ge(og_done, g - 1)
                part = slice(64 * half, 64 * half + 64)
                to = o_ps[n // 2]
                mm(to[part, 0:S], vv[:, 0, col:col + HD], probT[:, h % 2, 0:S], start=True, stop=False,
                   skip_group_check=True)
                ins = mm(to[part, P:S], vv[:, 1, col:col + HD], probT[:, h % 2, S:SW], start=False,
                         stop=True, skip_group_check=True)
                if n % 2:
                    ins.then_inc(pv_done, 1)

            def attend(st):
                transposes(st, 0)
                transposes(st, 1)
                values(st, 0)
                transposes(st, 2)
                values(st, 1)
                transposes(st, 3)
                values(st, 2)
                values(st, 3)

            def y_ready(st, ch):
                pe.wait_ge(ylo_done, st["first_y"] + (ch // 2 + 1 if ch < 4 else ch - 1)
                           if st["mixer"] == "pool" else st["first_y"] + ch + 1)

            def out_product(st, j, m, chunks, first, last):
                hi, lo = rows8(whi, st["u"] % NS), rows8(wlo, st["u"] % NS)
                at = slice(m * P, (m + 1) * P)
                for ch in chunks:
                    if j == 0 and m == 0:
                        y_ready(st, ch)
                    ins = split_product(acc[j % 2][:, m * S:(m + 1) * S], hi[:, ch, at], lo[:, ch, at], yhi[:, ch],
                                        ylo[:, ch], first and ch == chunks[0], last and ch == chunks[-1])
                return ins

            def out_rows(st, j, b, chunks, last):
                hi, lo = rows8(whi, st["u"] % NS), rows8(wlo, st["u"] % NS)
                tok = slice(b * P, (b + 1) * P)
                to = acc[j][:, b * S:(b + 1) * S]
                for ch in chunks:
                    if j == 0 and b == 0:
                        y_ready(st, ch)
                    mm(to, yhi[:, ch, tok], hi[:, ch], start=False, stop=False, skip_group_check=True)
                    mm(to, yhi[:, ch, tok], lo[:, ch], start=False, stop=False, skip_group_check=True)
                    ins = mm(to, ylo[:, ch, tok], hi[:, ch], start=False, stop=last and ch == chunks[-1],
                             skip_group_check=True)
                return ins

            def residual_rows(j):
                for b in range(2):
                    for n in range(2):
                        at = b * S + n * P
                        mm(acc[j][:, at:at + P], hT[:, 2 * j + n, b * P:(b + 1) * P], ident,
                           start=(b == 0 and n == 0), stop=False, skip_group_check=True)

            def out_step(st):
                kind, last_layer = st["kind"], st["mixer"] == "causal"
                j = st["i"]
                k = MIX_NORM[st["mixer"]] + 1
                early, late = range(0, 6), range(6, 8)
                if kind in ("OUTA", "OUT"):
                    pe.wait_ge(lo_done, st["u"] + 1)
                    pe.wait_ge(job_out, st["jobs"])
                if last_layer:
                    if kind == "OUTA":
                        residual_rows(0)
                        residual_rows(1)
                        out_rows(st, 0, 0, early, False)
                        out_rows(st, 0, 1, early, False)
                        return
                    if kind == "OUTB":
                        out_rows(st, 0, 0, late, True)
                        ins = out_rows(st, 0, 1, late, True)
                    else:
                        if j >= 2:
                            residual_rows(j)
                        out_rows(st, j, 0, range(DC), True)
                        ins = out_rows(st, j, 1, range(DC), True)
                    ins.then_inc(fin_mm, 1)
                    return
                if kind == "OUTA":
                    out_product(st, 0, 0, early, True, False)
                    out_product(st, 0, 1, early, False, False)
                    return
                if kind == "OUTB":
                    out_product(st, 0, 0, late, False, True).then_inc(delta, 1)
                    out_product(st, 0, 1, late, False, True).then_inc(delta, 1)
                else:
                    if j >= 2:
                        pe.wait_ge(res_done, DC * k + 2 * (j - 1))
                    for m in range(2):
                        out_product(st, j, m, range(DC), True, True).then_inc(delta, 1)
                        if 2 * j + m >= 2:
                            sum_squares(k, 2 * j + m - 2)

            def mixer(name):
                for st in PLANS[name]:
                    kind = st["kind"]
                    if st.get("job"):
                        job(st)
                    elif kind in ("ROTK", "ROTQ"):
                        rotate(st)
                    elif kind == "SC":
                        scores(st)
                    elif kind == "TPV":
                        attend(st)
                    elif kind in ("OUTA", "OUTB", "OUT"):
                        out_step(st)
                    elif kind == "MOD":
                        mod_sum(st["i"], mod2_ps[:, 0:2])
                        mod_sum(st["i"] + 1, mod2_ps[:, 2:4])

            def ffn(f):
                base, n0, k = FFN_UNIT[f], FB * f, FFN_NORM[f]

                def gate(u, i, reps=None, norm=None):
                    add = reps if reps is not None else 0
                    pe.wait_ge(lo_done, u + 1 + 3 * add)
                    if n0 + i > 0:
                        pe.wait_ge(silu_done, n0 + i + add)
                    project(sc[0], u % NS, norm).then_inc(ffn_used, 1)

                def up(u, i, reps=None):
                    add = reps if reps is not None else 0
                    pe.wait_ge(lo_done, u + 1 + 3 * add)
                    if n0 + i > 0:
                        pe.wait_ge(hid_done, n0 + i + add)
                    project(sc[1], u % NS).then_inc(ffn_used, 1)

                def down(u, i, reps=None):
                    add = reps if reps is not None else 0
                    hi, lo = rows2(whi, u % NS), rows2(wlo, u % NS)
                    pe.wait_ge(lo_done, u + 1 + 3 * add)
                    pe.wait_ge(hlo_done, n0 + i + 1 + add)
                    for m in range(DC):
                        for n in range(2):
                            at = slice(m * P, (m + 1) * P)
                            ins = split_product(acc[m // 2][:, (m % 2) * S:(m % 2 + 1) * S], hi[:, n, at], lo[:, n, at],
                                                hhi[:, n], hlo[:, n], False, False)
                        yield m, ins

                gate(base, 0, norm=k)
                up(base + 1, 0)
                for bank in acc:
                    mm(bank[:, :], zero_r[:, 0:P], zero_r[:, :], start=True, stop=False, skip_group_check=True)
                with pe.Fori(0, FB - 1) as j:
                    gate(base + 2, 1, reps=j)
                    up(base + 3, 1, reps=j)
                    for m, ins in down(base + 4, 0, reps=j):
                        if m == DC - 1:
                            ins.then_inc(ffn_used, 1)
                    if f == 0:
                        mod_sum(8, mod1_ps[:, 0:2], reps=j)
                        mod_sum(9, mod1_ps[:, 2:4], reps=j)
                if f == 0:
                    mod_sum(28, mod1_ps[:, 0:2])
                    mod_sum(29, mod1_ps[:, 2:4])
                for m, ins in down(base + 32, FB - 1):
                    ins.then_inc(delta, 1)
                    if m >= 3 and m % 2:
                        sum_squares(k + 1, m - 3)
                        sum_squares(k + 1, m - 2)
                sum_squares(k + 1, DC - 2)
                sum_squares(k + 1, DC - 1)

            pe.wait_ge(consts_in, 16)
            pe.wait_ge(rows_in, 128)
            nc.tensor.transpose(sc[0][:, 0:72], rowsA, ident[0:72, 0:72]).then_inc(rows_t, 1)
            nc.tensor.transpose(sc[0][:, 128:188], rowsB, ident[0:60, 0:60]).then_inc(rows_t, 1)
            pe.wait_ge(x_in, 16)
            for m in range(DC):
                for b in range(2):
                    at = (m % 2) * S + b * P
                    ins = nc.tensor.transpose(acc[m // 2][:, at:at + P], xo[:, b, m * P:(m + 1) * P], ident)
                ins.then_inc(x_t, 1)
            pe.wait_ge(set_done, 4)
            for a in range(MOD_START):
                if a == 4:
                    for m in range(DC):
                        sum_squares(0, m)
                mod_sum(a, mod0_ps[:, 2 * a:2 * a + 2])
            ffn(0)
            mixer("pool")
            sum_squares(2, DC - 2)
            sum_squares(2, DC - 1)
            ffn(1)
            for m in range(DC):
                sum_squares(4, m)
            mixer("window")
            sum_squares(5, DC - 2)
            sum_squares(5, DC - 1)
            mixer("causal")


tnum = {0: 0, 1: 1, 2: 2, 4: 3, 5: 4}
z_pairs = {"window": 4, "causal": 12}


def y_chunk(st, n):
    return st["local"] // 2 + n + (4 if st["mixer"] == "pool" else 0)


def heads_before_rotations():
    done = 0
    for name in ("pool", "window", "causal"):
        for st in PLANS[name]:
            if st["kind"] == "TPV":
                done = st["h"] + 4
            elif st["kind"] in ("ROTK", "ROTQ"):
                st["h_before"] = done


heads_before_rotations()

_INS = ["x", "c", "w_ada", "b_ada", "g_ffn1", "w1_gate", "w1_up", "w1_down", "g_mix", "w_in", "w_pool",
        "pool_scale", "w_out", "g_ffn2", "w2_gate", "w2_up", "w2_down", "g_final", "norm_g_2", "w_in_a_2",
        "sinks_a_2", "w_in_b_2", "w_out_2", "final_g_2"]


def kernel(**inputs):
    import concourse.bacc as _bacc
    from concourse.bass_utils import run_bass_kernel_spmd as _run

    nc = _bacc.Bacc("TRN2", target_bir_lowering=False, num_devices=1)
    arrays, args = {}, []
    for name in _INS:
        a = np.ascontiguousarray(inputs[name])
        arrays[f"in_{name}_dram"] = a
        args.append(nc.dram_tensor(f"in_{name}_dram", a.shape, mybir.dt.from_np(a.dtype), kind="ExternalInput").ap())
    arrays["shape_consts_dram"] = shape_constants()
    args.append(nc.dram_tensor("shape_consts_dram", (P, C_END), F32, kind="ExternalInput").ap())
    out = nc.dram_tensor("out_0_dram", (1, S, D), F32, kind="ExternalOutput").ap()
    build(nc, *args, out)
    r = _run(nc, [arrays], core_ids=[0])
    return r.results[0]["out_0_dram"]
```

```python
from contextlib import ExitStack

import numpy as np

import concourse.bass as bass
from concourse import mybir

F32 = mybir.dt.float32
F32R = mybir.dt.float32r
ALU = mybir.AluOpType
ACT = mybir.ActivationFunctionType
AX_X = mybir.AxisListType.X

P = 128
S = 256
D = 1024
DC = D // P
F = 2816
UC = 256
UNIT = DC * UC
FB = F // UC
NS = 3
HD = 64
NEG = -1e30
EPS1, EPS2 = 1e-6, 1e-5
SCALE = HD ** -0.5
MOD_UNITS = 9 * D // UC
MOD_START = 2 * D // UC
SW = 384

C_IDENT, C_ROT, C_DIST, C_MULT, C_WIN, C_CAUSAL = 0, 128, 256, 640, 1024, 1408
C_COS, C_SIN, C_COUNT, C_END = 1792, 2048, 2304, 2368


def shape_constants():
    out = np.zeros((P, C_END), np.float32)
    out[:, C_IDENT:C_IDENT + P] = np.eye(P)
    for m in range(P):
        if m % HD < HD // 2:
            out[m + HD // 2, C_ROT + m] = -1.0
        else:
            out[m - HD // 2, C_ROT + m] = 1.0
    q = np.arange(P)[:, None]
    d = np.concatenate([q - np.arange(P)[None], P + q - np.arange(S)[None]], axis=1)
    out[:, C_DIST:C_DIST + SW] = np.maximum(d, 0)
    times = (d <= 128).astype(int) + (d % 4 == 0) + (d % 16 == 0)
    times = np.where(d >= 0, times, 0)
    out[:, C_MULT:C_MULT + SW] = np.where(times > 0, np.log(np.maximum(times, 1)), NEG)
    out[:, C_WIN:C_WIN + SW] = np.where((d >= 0) & (d < 128), 0.0, NEG)
    out[:, C_CAUSAL:C_CAUSAL + SW] = np.where(d >= 0, 0.0, NEG)
    inv = np.float32(10000.0) ** (-np.arange(0, HD, 2, dtype=np.float32) / np.float32(HD))
    ang = np.arange(S, dtype=np.float32)[None] * inv.astype(np.float32)[np.arange(P) % (HD // 2)][:, None]
    out[:, C_COS:C_COS + S] = np.cos(ang)
    out[:, C_SIN:C_SIN + S] = np.sin(ang)
    for g in range(4):
        w = 2 ** (g + 1)
        out[:, C_COUNT + 16 * g:C_COUNT + 16 * (g + 1)] = w / np.minimum(np.arange(16) + 1, w)
    return out


MIX_NORM = {"pool": 1, "window": 4, "causal": 5}


def mixer_plan():
    u, p, r, h, g, y, z = 3 * FB, 0, 0, 0, 0, 0, 0
    mods = MOD_START
    plans = {}
    for name in ("pool", "window", "causal"):
        steps = []
        first_job, first_head, first_pair, first_y, first_rot = p, h, g, y, r
        if name == "pool":
            order = ["U0", "MAC20", "U1", "K0", "MOD20", "MAC22", "K1", "V0", "MOD22", "MAC24", "Q0", "V1",
                     "SC0", "W0", "W1", "MOD24", "MAC26", "Q1", "TPV0", "SC1", "OUTA", "MOD26", "TPV1", "MAC28",
                     "OUTB", "OUT1", "MOD28", "MAC30", "OUT2", "MOD30", "OUT3"]
        else:
            order = ["KV0", "Q0"] if name == "window" else ["K0", "V0", "Q0"]
            order += ["ROTK", "ROTQ", "Z0", "SC0"]
            for i in range(1, 4):
                order += [f"Q{i}", f"TPV{i - 1}", "ROTQ", f"Z{i}", f"SC{i}"]
            order += ["OUTA", "TPV3", "OUTB", "OUT1", "OUT2", "OUT3"]
        for what in order:
            kind, i = what.rstrip("0123456789"), what.lstrip("ABCDEFGHIJKLMNOPQRSTUVWXYZ")
            i = int(i) if i else 0
            st = dict(kind=kind, i=i, mixer=name)
            if kind in ("U", "K", "V", "KV", "Q", "Z", "W"):
                st.update(job=True, p=p, first=p == first_job)
                if kind == "Q":
                    q = p
                p += 1
                st["zs"] = z
                z += kind == "Z"
                if kind == "W":
                    st["y"] = y
                    y += 1
                else:
                    st["u"] = u
                    u += 1
            elif kind in ("ROTK", "ROTQ"):
                st.update(r=r, p=p - 1 if kind == "ROTQ" else first_job)
                r += 1
            elif kind == "SC":
                st.update(h=h, local=h - first_head, rots=r, mods=mods, q=q)
                h += 4
            elif kind == "MOD":
                st["h"] = h
                mods = i + 2
            elif kind == "TPV":
                st.update(h=first_head + 4 * i, g=g, y=y, local=4 * i)
                g += 2
                y += 2
            elif kind in ("OUTA", "OUTB", "OUT"):
                st["u"] = u
                st["first_y"] = first_y
                if kind != "OUTA":
                    u += 1
            st["jobs"] = p
            st["zs_all"] = z
            steps.append(st)
        for st, after in zip(steps, steps[1:]):
            st["next"] = after
        if name == "pool":
            u += 3 * FB
        plans[name] = steps
    assert u == 3 * FB + 12 + 3 * FB + 13 + 14
    return plans, u


PLANS, UNITS = mixer_plan()

ADA_SLOT = {a: 1 if 9 <= a < 20 else a % 2 for a in range(MOD_START, MOD_UNITS)}


def ada_landings(a):
    return 16 * sum(ADA_SLOT[n] == ADA_SLOT[a] for n in range(MOD_START, a + 1))


def by_act(a):
    return (a < MOD_START or 20 <= a < 32) and a % 2 == 1 or a == 22


def products(a, act):
    return sum(by_act(n) == act for n in range(a + 1))


def slot_before(a):
    return max([n for n in range(MOD_START, a) if ADA_SLOT[n] == ADA_SLOT[a]], default=-1) + 1


FFN_UNIT = (0, 3 * FB + 12)
FFN_NORM = (0, 2)
RESIDUAL = {1: 0, 2: 1, 3: 2, 5: 3}


def build(nc, x, c, w_ada, b_ada, g_ffn1, w1_gate, w1_up, w1_down, g_mix, w_in, w_pool, pool_scale, w_out,
          g_ffn2, w2_gate, w2_up, w2_down, g_final, norm_g_2, w_in_a_2, sinks_a_2, w_in_b_2, w_out_2,
          final_g_2, shape_consts, out):
    with ExitStack() as ctx:
        def sb(name, shape, dt=F32):
            return ctx.enter_context(nc.sbuf_tensor(name, shape, dt))

        def sem(name):
            return ctx.enter_context(nc.semaphore(name))

        raw = sb("raw", [P, NS, UNIT])
        whi = sb("whi", [P, NS, UNIT], F32R)
        wlo = sb("wlo", [P, NS, UNIT], F32R)
        ada = sb("ada", [P, 2, DC, UC])
        macc = sb("macc", [P, 2, UC])
        hT = sb("hT", [P, DC, S])
        nhi = sb("nhi", [P, DC, S], F32R)
        nlo = sb("nlo", [P, DC, S], F32R)
        sq = sb("sq", [P, 4, S])
        tn = sb("tn", [P, 4, S])
        std = sb("std", [P, S])
        rstd = sb("rstd", [P, S])
        xo = sb("xo", [P, 2, D])
        tmp = sb("tmp", [P, 4, S + 8])
        hhi = sb("hhi", [P, 2, S], F32R)
        hlo = sb("hlo", [P, 2, S], F32R)
        pw = sb("pw", [P, 2, S + 8])
        kraw = sb("kraw", [P, 2, S])
        kd = sb("kd", [P, 4, S])
        qraw = sb("qraw", [P, 2, S])
        qT = sb("qT", [P, 2, S])
        vv = sb("vv", [P, 2, 512])
        sz = sb("sz", [P, 2, S])
        prob = sb("prob", [P, 4, SW])
        probT = sb("probT", [P, 2, SW])
        alibi = sb("alibi", [P, 2, SW])
        og = sb("og", [P, 2, S])
        yhi = sb("yhi", [P, DC, S], F32R)
        ylo = sb("ylo", [P, DC, S], F32R)
        consts = sb("consts", [P, C_END])
        ones = sb("ones", [P, P])
        zero_r = sb("zero_r", [P, 512], F32R)
        wpool = sb("wpool", [P, 4, P])
        biasT = sb("biasT", [P, 72])
        gainT = sb("gainT", [P, 60])
        cT = sb("cT", [P, DC])
        mod = sb("mod", [P, 72])
        coefA = sb("coefA", [P, 3, DC])
        gate_h = sb("gate_h", [P, 2, DC])
        sinks = sb("sinks", [P, 16])
        fgain = sb("fgain", [P, D])
        tiny = sb("tiny", [P, 4])
        junk = sb("junk", [P, 8])
        mx = sb("mx", [P, 4, 2])
        nm = sb("nm", [P, 4, 2])
        den = sb("den", [P, 4, 2])
        esink = sb("esink", [P, 4, 2])
        rden = sb("rden", [P, 4, 2])
        fss = sb("fss", [P, 2, 4])
        fst = sb("fst", [P, 3, 2])
        acc = [ctx.enter_context(nc.psum_tensor(f"acc{i}", [P, 512], F32)) for i in range(4)]
        sc = [ctx.enter_context(nc.psum_tensor(f"sc{i}", [P, 512], F32)) for i in range(2)]
        tp0 = ctx.enter_context(nc.psum_tensor("tp0", [P, 512], F32))
        stat = ctx.enter_context(nc.psum_tensor("stat", [P, 512], F32))
        tp = [tp0, acc[2]]
        rot_ps = acc[2]
        o_ps = [acc[3], stat]
        ss_ps = stat[:, 0:S]
        mod0_ps, mod1_ps, mod2_ps = sc[1][:, 0:16], stat[:, S:S + 4], sc[0][:, 0:4]

        rope_c, rope_s = tn[:, 0:2], tn[:, 2:4]
        rowsA = kd[0:72, 0, 0:P]
        rowsB = kd[0:60, 1, 0:P]
        ident = consts[:, C_IDENT:C_IDENT + P]
        rotation = consts[:, C_ROT:C_ROT + P]
        cos2 = consts[:, C_COS:C_COS + S].unsqueeze(1).to_broadcast([P, 2, S])
        sin2 = consts[:, C_SIN:C_SIN + S].unsqueeze(1).to_broadcast([P, 2, S])
        cos1, sin1 = consts[:, C_COS:C_COS + S], consts[:, C_SIN:C_SIN + S]
        silu_g = tmp[:, 0:2, 0:S]
        hidden = tmp[:, 2:4, 0:S]
        start_slots = [ada[:, 0], ada[:, 1]] + [raw[:, n, :].rearrange("p (c n) -> p c n", c=DC) for n in (2, 0, 1)]
        c_mul = cT[:, :].unsqueeze(2).to_broadcast([P, DC, UC])

        landed = [sem(f"landed{s}") for s in range(NS)]
        hi_done = sem("hi_done")
        lo_done = sem("lo_done")
        ffn_used = sem("ffn_used")
        consts_in = sem("consts_in")
        wpool_in = sem("wpool_in")
        tables_in = sem("tables_in")
        late_in = sem("late_in")
        rows_in = sem("rows_in")
        x_in = sem("x_in")
        ada0_in = [sem(f"ada0_in{s}") for s in range(5)]
        ada_in = [sem(f"ada_in{s}") for s in range(2)]
        set_done = sem("set_done")
        rows_t = sem("rows_t")
        gains_done = sem("gains_done")
        c_done = sem("c_done")
        x_t = sem("x_t")
        prod_done = sem("prod_done")
        aprod_done = sem("aprod_done")
        macc_done = sem("macc_done")
        mod_cols = sem("mod_cols")
        mod_done = sem("mod_done")
        res_done = sem("res_done")
        sq_done = sem("sq_done")
        sqs_done = sem("sqs_done")
        ss_done = sem("ss_done")
        std_done = sem("std_done")
        t_done = sem("t_done")
        nhi_done = sem("nhi_done")
        nlo_done = sem("nlo_done")
        silu_done = sem("silu_done")
        hid_done = sem("hid_done")
        hhi_done = sem("hhi_done")
        hlo_done = sem("hlo_done")
        delta = sem("delta")
        job_done = sem("job_done")
        job_out = sem("job_out")
        z_done = sem("z_done")
        rot_done = sem("rot_done")
        rope_done = sem("rope_done")
        kd_done = sem("kd_done")
        pooled = sem("pooled")
        alibi_done = sem("alibi_done")
        sc_done = sem("sc_done")
        sm_read = sem("sm_read")
        nm_done = sem("nm_done")
        ex_done = sem("ex_done")
        p_done = sem("p_done")
        tp_done = sem("tp_done")
        pt_done = sem("pt_done")
        pv_done = sem("pv_done")
        og_done = sem("og_done")
        yhi_done = sem("yhi_done")
        ylo_done = sem("ylo_done")
        fin_mm = sem("fin_mm")
        fss_done = sem("fss_done")
        fstd_done = sem("fstd_done")
        fsum_done = sem("fsum_done")
        res_out = sem("res_out")
        out_sent = sem("out_sent")
        dve_step = sem("dve_step")
        act_step = sem("act_step")
        pool_step = sem("pool_step")

        block = ctx.enter_context(nc.Block())

        def rows8(t, s):
            return t[:, s, :].rearrange("p (c n) -> p c n", c=DC)

        def rows2(t, s):
            return t[:, s, :].rearrange("p (c n) -> p c n", c=2)

        def by_chunk(w):
            return w.rearrange("(c p) n -> p c n", p=P)

        w_ada_v = by_chunk(w_ada[0])
        ffn_w = [(by_chunk(w1_gate[0]), by_chunk(w1_up[0]), by_chunk(w1_down[0])),
                 (by_chunk(w2_gate[0]), by_chunk(w2_up[0]), by_chunk(w2_down[0]))]
        in_w = {"pool": by_chunk(w_in[0]), "window": by_chunk(w_in_a_2[0]), "causal": by_chunk(w_in_b_2[0])}
        out_w = {"pool": by_chunk(w_out[0]), "window": by_chunk(w_out_2[0]), "causal": by_chunk(w_out_2[1])}
        first_col = {"pool": dict(U=0, Q=512, K=1024, V=1536), "window": dict(Q=0, KV=1024, Z=1280),
                     "causal": dict(Q=0, K=1024, V=1280, Z=1536)}
        gain_col = {0: 0, 1: 8, 2: 16, 3: 24, 4: 32, 5: 40}

        def norm_gain(k, m):
            return coefA[:, k, m:m + 1] if k < 3 else gainT[:, gain_col[k] + m:gain_col[k] + m + 1]

        def norm_shift(k, m):
            return mod[:, 24 * k + m:24 * k + m + 1] if k < 3 else tiny[:, 2:3]

        def head_place(mixer, local):
            kv = {"pool": local // 2, "window": local // 8, "causal": local // 4}[mixer]
            v = {"pool": local, "window": local // 8, "causal": local // 4}[mixer]
            return local % 2, kv, HD * v

        @block.sync
        def _(sp):
            def load_unit(u, view, add=0, reps=None):
                if u >= NS or reps is not None:
                    sp.wait_ge(lo_done, u - NS + 1 + (3 * reps if reps is not None else 0))
                sp.dma_start(raw[:, u % NS, :].rearrange("p (c n) -> p c n", c=view.shape[1]),
                             view).then_inc(landed[u % NS], 16)

            def load_ada(a, reps=None):
                col = a * UC if reps is None else reps * UC + a * UC
                if slot_before(a):
                    sp.wait_ge(macc_done, slot_before(a) + (reps if reps is not None else 0))
                sp.dma_start(ada[:, ADA_SLOT[a]], w_ada_v[:, :, bass.ds(col, UC)]).then_inc(ada_in[ADA_SLOT[a]], 16)

            sp.dma_start(rowsB[52:60, :], c.rearrange("a (k p) -> (a k) p", p=P)).then_inc(rows_in, 16)
            sp.dma_start(rowsB[0:8, :], g_ffn1.rearrange("a (k p) -> (a k) p", p=P)).then_inc(rows_in, 16)
            sp.dma_start(consts[:, 0:P], shape_consts[:, 0:P]).then_inc(consts_in, 16)
            sp.dma_start(rowsA, b_ada.rearrange("a (k p) -> (a k) p", p=P)).then_inc(rows_in, 16)
            sp.dma_start(xo[:, :, :], x[0].rearrange("(b p) n -> p b n", p=P)).then_inc(x_in, 16)
            for a in range(MOD_START):
                if a >= 5:
                    sp.wait_ge(macc_done, a - 4)
                sp.dma_start(start_slots[a % 5], w_ada_v[:, :, a * UC:(a + 1) * UC]).then_inc(ada0_in[a % 5], 16)
            sp.wait_ge(macc_done, 4)
            load_unit(0, ffn_w[0][0][:, :, 0:UC])
            sp.wait_ge(macc_done, 5)
            load_unit(1, ffn_w[0][1][:, :, 0:UC])
            sp.wait_ge(macc_done, 6)
            load_ada(8)
            sp.wait_ge(macc_done, MOD_START)
            for f in range(2):
                base = FFN_UNIT[f]
                gate, up, down = ffn_w[f]
                if f == 1:
                    load_unit(base, gate[:, :, 0:UC])
                    load_unit(base + 1, up[:, :, 0:UC])
                    load_ada(32)
                    load_ada(33)
                first = f == 0
                if first:
                    sp.dma_start(rows8(raw, 2), gate[:, :, UC:2 * UC]).then_inc(landed[2], 16)
                    load_ada(9)
                    load_unit(3, up[:, :, UC:2 * UC])
                    load_unit(4, down[:, 0:2, :])
                    sp.dma_start(consts[:, P:C_END], shape_consts[:, P:C_END]).then_inc(tables_in, 16)
                for start, end in ((1, FB - 1),) if first else ((0, 4), (4, FB - 1)):
                    with sp.Fori(start, end) as j:
                        u = base + 2
                        load_unit(u, gate[:, :, bass.ds(j * UC + UC, UC)], reps=j)
                        load_unit(u + 1, up[:, :, bass.ds(j * UC + UC, UC)], reps=j)
                        load_unit(u + 2, down[:, bass.ds(j * 2, 2), :], reps=j)
                        if first:
                            load_ada(10, reps=j - 1)
                    if end == 4:
                        load_ada(34)
                        load_ada(35)
                load_unit(base + 32, down[:, 2 * (FB - 1):2 * FB, :])
                if first:
                    sp.dma_start(wpool[:, :, :], w_pool[0].rearrange("g c d -> c g d")).then_inc(wpool_in, 16)
                    ada_after = {3 * FB: (19,), 3 * FB + 1: (20,), 3 * FB + 2: (21,), 3 * FB + 5: (22, 23), 3 * FB + 7: (24, 25),
                                 3 * FB + 9: (26, 27), 3 * FB + 10: (28, 29), 3 * FB + 11: (30, 31)}
                for name in ("pool",) if first else ("window", "causal"):
                    for st in PLANS[name]:
                        if "u" not in st or st["kind"] == "OUTA":
                            continue
                        n = st["i"] if st["kind"] != "OUTB" else 0
                        if st["kind"] in ("OUTB", "OUT"):
                            load_unit(st["u"], out_w[name][:, :, n * UC:(n + 1) * UC])
                        else:
                            at = first_col[name][st["kind"]] + n * UC
                            load_unit(st["u"], in_w[name][:, :, at:at + UC])
                        for a in ada_after.get(st["u"], ()):
                            load_ada(a)
                if first:
                    sp.dma_start(fgain[:, :], final_g_2.rearrange("(a n) -> a n", a=1).to_broadcast([P, D])
                                 ).then_inc(late_in, 16)
                    sp.dma_start(sinks[:, :], sinks_a_2.to_broadcast([P, 16])).then_inc(late_in, 16)
            for j in range(4):
                sp.wait_ge(res_out, j + 1)
                sp.dma_start(out[0].rearrange("(b p) n -> p b n", p=P)[:, :, j * UC:(j + 1) * UC],
                             xo[:, :, j * UC:(j + 1) * UC]).then_inc(out_sent, 16)
            sp.wait_ge(out_sent, 64)

        @block.gpsimd
        def _(pool):
            steps = [0]

            def link(ins):
                steps[0] += 1
                ins.then_inc(pool_step, 1)
                pool.wait_ge(pool_step, steps[0])

            def product(a, reps=None):
                to = ada[:, ADA_SLOT[a]]
                pool.wait_ge(ada_in[ADA_SLOT[a]], ada_landings(a) + (16 * reps if reps is not None else 0))
                nc.gpsimd.tensor_tensor(to, to, c_mul, ALU.mult).then_inc(prod_done, 1)

            def add_squares(k):
                for m in range(1, 4):
                    pool.wait_ge(sq_done, DC * k + m + 1)
                    if m > 1:
                        pool.wait_ge(sqs_done, 3 * (k - 1) + m - 1)
                    first = sq[:, 0] if m == 1 else std[:, :]
                    nc.gpsimd.tensor_tensor(std[:, :], first, sq[:, m], ALU.add).then_inc(sqs_done, 1)

            nc.gpsimd.memset(ones[:, :], 1.0).then_inc(set_done, 1)
            nc.gpsimd.memset(zero_r[:, :].bitcast(F32), 0.0).then_inc(set_done, 1)
            nc.gpsimd.memset(pw[:, :, :], 0.0).then_inc(set_done, 1)
            pool.wait_ge(c_done, 1)
            for a in range(MOD_START):
                if not by_act(a):
                    pool.wait_ge(ada0_in[a % 5], 16 * (a // 5 + 1))
                    nc.gpsimd.tensor_tensor(start_slots[a % 5], start_slots[a % 5], c_mul,
                                            ALU.mult).then_inc(prod_done, 1)
            pool.wait_ge(hi_done, 1)
            nc.gpsimd.tensor_tensor(wlo[:, 0], raw[:, 0], whi[:, 0].bitcast(F32), ALU.subtract).then_inc(lo_done, 1)
            product(8)
            product(9)
            with pool.Fori(0, FB - 1) as j:
                product(10, reps=j)

            def bias(h):
                if h >= 2:
                    pool.wait_ge(sm_read, h - 1)
                slope = 2.0 ** (-8.0 * (h + 1) / 8)
                link(nc.gpsimd.tensor_scalar(alibi[:, h % 2], consts[:, C_DIST:C_DIST + SW], -slope, None, ALU.mult))
                nc.gpsimd.tensor_tensor(alibi[:, h % 2], alibi[:, h % 2], consts[:, C_MULT:C_MULT + SW],
                                        ALU.add).then_inc(alibi_done, 1)

            def pooling(g):
                src = tmp[:, g]
                own = tmp[:, g, 8:8 + S]
                for i in range(g + 1):
                    to = pw[:, i % 2]
                    link(nc.gpsimd.tensor_tensor(to[:, 8:8 + S], src[:, 8:8 + S], src[:, 8 - 2 ** i:8 - 2 ** i + S],
                                                 ALU.add))
                    src = to
                win = src[:, 8:8 + S]
                link(nc.gpsimd.tensor_scalar(win, win, 1.0 / 2 ** (g + 1), None, ALU.mult))
                link(nc.gpsimd.tensor_tensor(win[:, 0:16], win[:, 0:16],
                                             consts[:, C_COUNT + 16 * g:C_COUNT + 16 * (g + 1)], ALU.mult))
                ins = nc.gpsimd.tensor_tensor(own, win, own, ALU.subtract)
                ins.then_inc(pooled, 1)
                pool.wait_ge(pooled, g + 1)

            product(20)
            add_squares(1)
            pool.wait_ge(tables_in, 16)
            bias(0)
            bias(1)
            pool.wait_ge(hlo_done, FB)
            link(nc.gpsimd.memset(tmp[:, :, 0:8], 0.0))
            for st in PLANS["pool"]:
                if st["kind"] == "U":
                    pool.wait_ge(job_out, st["p"] + 1)
                    pooling(2 * st["i"])
                    pooling(2 * st["i"] + 1)
                elif st["kind"] == "SC":
                    for h in range(max(2, 4 * st["i"]), 4 * st["i"] + 4):
                        bias(h)
                elif st["kind"] == "MAC" and st["i"] > 20 and not by_act(st["i"]):
                    product(st["i"])
            add_squares(2)
            for a in range(32, MOD_UNITS):
                product(a)
            for k in range(3, 6):
                add_squares(k)

        @block.scalar
        def _(act):
            def high(u, reps=None, by=None):
                if u >= UNITS:
                    return
                n = 16 * (u // NS + 1)
                act.wait_ge(landed[u % NS], n + 16 * reps if reps is not None else n)
                nc.scalar.activation(whi[:, u % NS], raw[:, u % NS], ACT.Copy).then_inc(hi_done, 1)

            def squares(k, chunks=range(DC)):
                for m in chunks:
                    act.wait_ge(res_done, DC * k + m + 1)
                    if m >= 4:
                        if k == 0:
                            act.wait_ge(ss_done, m - 3)
                        else:
                            act.wait_ge(sqs_done, 3 * (k - 1) + max(m - 4, 1))
                    nc.scalar.activation(sq[:, m % 4], hT[:, m], ACT.Square).then_inc(sq_done, 1)

            def load_sqrt(n):
                nc.scalar.activation(junk[:, n:n + 1], tiny[:, 0:1], ACT.Sqrt)

            def deviation(k):
                act.wait_ge(ss_done, DC + 5 * k)
                eps = tiny[:, 0:1] if k <= 3 else tiny[:, 1:2]
                nc.scalar.activation(std[:, :], ss_ps, ACT.Sqrt, bias=eps, scale=1.0 / D).then_inc(std_done, 1)

            def norm_high(k):
                for m in range(DC):
                    act.wait_ge(t_done, DC * tnum[k] + m + 1)
                    nc.scalar.activation(nhi[:, m], tn[:, m % 4], ACT.Identity,
                                         bias=norm_shift(k, m)).then_inc(nhi_done, 1)

            def product(a):
                if a < MOD_START:
                    to = start_slots[a % 5]
                    act.wait_ge(ada0_in[a % 5], 16 * (a // 5 + 1))
                else:
                    to = ada[:, ADA_SLOT[a]]
                    act.wait_ge(ada_in[ADA_SLOT[a]], ada_landings(a))
                for ch in range(DC):
                    ins = nc.scalar.activation(to[:, ch], to[:, ch], ACT.Copy, scale=cT[:, ch:ch + 1])
                ins.then_inc(aprod_done, 1)

            def job(st):
                act.wait_ge(job_done, st["p"] + 1)
                bank = acc[st["p"] % 2]
                pair = bank[:, :].rearrange("p (b n) -> p b n", b=2)
                kind, i, mixer = st["kind"], st["i"], st["mixer"]
                if kind == "U":
                    ins = nc.scalar.activation(tmp[:, 2 * i:2 * i + 2, 8:8 + S], pair, ACT.Copy)
                elif kind == "K":
                    to = kd[:, 2 * i:2 * i + 2] if mixer == "pool" else kraw[:, :, :]
                    ins = nc.scalar.activation(to, pair, ACT.Copy)
                elif kind == "V":
                    ins = nc.scalar.activation(vv[:, :, UC * i:UC * (i + 1)], pair, ACT.Copy)
                elif kind == "KV":
                    nc.scalar.activation(kraw[:, 0], bank[:, 0:S], ACT.Copy)
                    ins = nc.scalar.activation(vv[:, :, 0:P], bank[:, S:2 * S].rearrange("p (b n) -> p b n", b=2),
                                               ACT.Copy)
                elif kind == "Q":
                    ins = nc.scalar.activation(qT[:, :, :] if mixer == "pool" else qraw[:, :, :], pair, ACT.Copy,
                                               scale=SCALE)
                elif kind == "Z":
                    if i:
                        act.wait_ge(og_done, z_pairs[mixer] + 2 * i)
                    ins = nc.scalar.activation(sz[:, :, :], pair, ACT.Tanh, scale=0.5)
                else:
                    if i:
                        act.wait_ge(ylo_done, st["y"])
                    for n in range(2):
                        ch = 48 + 2 * i + n
                        ins = nc.scalar.activation(kraw[:, n], pair[:, n], ACT.Copy, scale=gainT[:, ch:ch + 1])
                ins.then_inc(job_out, 1)
                if kind == "Z" or (kind == "Q" and st["next"]["kind"] == "TPV"):
                    return
                if kind == "W":
                    act.wait_ge(job_out, st["p"] + 1)
                    nc.scalar.activation(yhi[:, 2 * i:2 * i + 2], kraw[:, :, :], ACT.Copy).then_inc(yhi_done, 1)
                else:
                    high(st["u"] + NS)

            def duplicate(st):
                act.wait_ge(rope_done, st["r"] + 1)
                for half in range(2):
                    for src in range(2):
                        if st["mixer"] == "window":
                            to, of = kd[64 * half:64 * half + 64, src], kraw[64 * src:64 * src + 64, 0]
                        else:
                            to, of = kd[64 * half:64 * half + 64, src::2], kraw[64 * src:64 * src + 64, :]
                        ins = nc.scalar.activation(to, of, ACT.Copy)
                ins.then_inc(kd_done, 1)

            def softmax(st):
                for n in range(4):
                    h = st["h"] + n
                    s = h % 4
                    act.wait_ge(nm_done, h + 1)
                    if st["mixer"] == "window":
                        head = st["local"] + n
                        nc.scalar.activation(esink[:, s], nm[:, s], ACT.Exp, bias=sinks[:, head:head + 1])
                    for b, (lo, up) in enumerate(((0, P), (P, SW))):
                        ins = nc.scalar.activation(prob[:, s, lo:up], prob[:, s, lo:up], ACT.Exp,
                                                   bias=nm[:, s, b:b + 1], accum_out=den[:, s, b:b + 1])
                    ins.then_inc(ex_done, 1)

            def probabilities(st, n):
                h = st["h"] + n
                act.wait_ge(tp_done, h + 1)
                nc.scalar.activation(probT[:, h % 2], tp[h % 2][:, 0:SW], ACT.Copy).then_inc(pt_done, 1)

            def outputs(st, early):
                if not early:
                    probabilities(st, 0)
                    probabilities(st, 1)
                for n in range(2):
                    probabilities(st, n + 2)
                    g = st["g"] + n
                    act.wait_ge(og_done, g + 1)
                    nc.scalar.activation(yhi[:, y_chunk(st, n)], og[:, g % 2], ACT.Copy).then_inc(yhi_done, 1)

            def mixer(name):
                before = None
                for st in PLANS[name]:
                    if st["kind"] == "Q" and st["next"]["kind"] == "TPV":
                        probabilities(st["next"], 0)
                        probabilities(st["next"], 1)
                    if st.get("job"):
                        job(st)
                    elif st["kind"] == "ROTK":
                        duplicate(st)
                    elif st["kind"] == "SC":
                        softmax(st)
                        if before["kind"] == "Z":
                            high(before["u"] + NS)
                    elif st["kind"] == "TPV":
                        early = before["kind"] == "Q"
                        outputs(st, early)
                        if early:
                            high(before["u"] + NS)
                    elif st["kind"] in ("OUTB", "OUT"):
                        j = st["i"]
                        if name == "causal":
                            act.wait_ge(fin_mm, j + 1)
                        else:
                            k = MIX_NORM[name] + 1
                            act.wait_ge(delta, DC * RESIDUAL[k] + 2 * j + 2)
                            if j == 0:
                                load_sqrt(k)
                            squares(k, range(2 * j, 2 * j + 2))
                        if j < 3 or name == "causal":
                            high(st["u"] + NS)
                    elif st["kind"] == "MAC":
                        if by_act(st["i"]):
                            product(st["i"])
                        product(st["i"] + 1)
                    before = st

            def ffn(f):
                base, n0 = FFN_UNIT[f], FB * f
                done = (FB * 3 - 1) * f

                def silu(i, reps=None):
                    add = reps if reps is not None else 0
                    if n0 + i > 0:
                        act.wait_ge(hid_done, n0 + i + add)
                    nc.scalar.activation(silu_g, sc[0][:, :].rearrange("p (b n) -> p b n", b=2),
                                         ACT.Silu).then_inc(silu_done, 1)

                def hidden_high(i, reps=None):
                    act.wait_ge(hid_done, n0 + i + 1 + (reps if reps is not None else 0))
                    nc.scalar.activation(hhi[:, :, :], hidden, ACT.Copy).then_inc(hhi_done, 1)

                act.wait_ge(ffn_used, done + 1)
                silu(0)
                high(base + 3)
                act.wait_ge(ffn_used, done + 2)
                high(base + 4)
                hidden_high(0)
                with act.Fori(0, FB - 1) as j:
                    u = base + 2
                    act.wait_ge(ffn_used, 3 * j + (done + 3))
                    silu(1, reps=j)
                    high(u + 3, reps=j)
                    act.wait_ge(ffn_used, 3 * j + (done + 4))
                    high(u + 4, reps=j)
                    act.wait_ge(ffn_used, 3 * j + (done + 5))
                    hidden_high(1, reps=j)
                    high(u + 5, reps=j)
                load_sqrt(FFN_NORM[f] + 1)
                squares(FFN_NORM[f] + 1)

            for at, g in ((8, g_mix), (16, g_ffn2), (32, norm_g_2), (48, pool_scale)):
                rows = g.rearrange("a (k p) -> (a k) p", p=P)
                act.dma_start(rowsB[at:at + rows.shape[0], :], rows).then_inc(rows_in, 16)
            act.dma_start(rowsB[24:32, :], g_final.rearrange("(k p) -> k p", p=P)).then_inc(rows_in, 16)
            act.wait_ge(gains_done, 2)
            nc.scalar.activation(cT[:, :], gainT[:, 52:60], ACT.Silu).then_inc(c_done, 1)
            act.wait_ge(set_done, 4)
            act.wait_ge(c_done, 1)
            load_sqrt(0)
            squares(0)
            product(1)
            deviation(0)
            product(3)
            product(5)
            product(7)
            high(0)
            norm_high(0)
            high(1)
            high(2)
            ffn(0)
            deviation(1)
            norm_high(1)
            high(FFN_UNIT[0] + 3 * FB + 2)
            mixer("pool")
            deviation(2)
            norm_high(2)
            high(FFN_UNIT[1] + 2)
            ffn(1)
            deviation(3)
            high(FFN_UNIT[1] + 3 * FB + 2)
            squares(4)
            deviation(4)
            norm_high(4)
            act.wait_ge(late_in, 32)
            mixer("window")
            deviation(5)
            norm_high(5)
            high(PLANS["causal"][0]["u"] + 2)
            mixer("causal")
            load_sqrt(7)
            for j in range(4):
                act.wait_ge(fin_mm, j + 1)
                for b in range(2):
                    ins = nc.scalar.activation((sq, tn)[j // 2][:, 2 * (j % 2) + b], acc[j][:, b * S:(b + 1) * S], ACT.Square,
                                               accum_out=fss[:, b, j:j + 1])
                ins.then_inc(fss_done, 1)
            act.wait_ge(fsum_done, 1)
            nc.scalar.activation(fst[:, 1], fst[:, 0], ACT.Sqrt, bias=tiny[:, 1:2], scale=1.0 / D).then_inc(fstd_done, 1)

        @block.vector
        def _(dve):
            steps = [0]

            def link(ins):
                steps[0] += 1
                ins.then_inc(dve_step, 1)
                dve.wait_ge(dve_step, steps[0])

            def low(u, reps=None):
                if u >= UNITS:
                    return
                dve.wait_ge(hi_done, u + 1 + (3 * reps if reps is not None else 0))
                nc.vector.tensor_tensor(wlo[:, u % NS], raw[:, u % NS], whi[:, u % NS].bitcast(F32),
                                        ALU.subtract).then_inc(lo_done, 1)

            def residual(k, chunks=range(DC)):
                for m in chunks:
                    dve.wait_ge(delta, DC * RESIDUAL[k] + 2 * (m // 2) + 2)
                    bank = acc[m // 2] if k in (1, 3) else acc[(m // 2) % 2]
                    upd = bank[:, (m % 2) * S:(m % 2 + 1) * S]
                    if k == 5:
                        ins = nc.vector.tensor_tensor(hT[:, m], upd, hT[:, m], ALU.add)
                    else:
                        gate = mod[:, 40 + m:41 + m] if k == 2 else gate_h[:, k // 2, m:m + 1]
                        ins = nc.vector.scalar_tensor_tensor(out=hT[:, m], in0=upd, scalar=gate, in1=hT[:, m],
                                                             op0=ALU.mult, op1=ALU.add)
                    ins.then_inc(res_done, 1)

            def inverse_deviation(k):
                dve.wait_ge(std_done, k + 1)
                link(nc.vector.reciprocal(rstd[:, :], std[:, :]))

            def normalise(k):
                if k > 0:
                    inverse_deviation(k)
                for m in range(DC + 1):
                    if m < DC:
                        if k == 3:
                            nc.vector.scalar_tensor_tensor(out=hT[:, m], in0=hT[:, m], scalar=norm_gain(k, m),
                                                           in1=rstd[:, :], op0=ALU.mult,
                                                           op1=ALU.mult).then_inc(res_done, 1)
                            continue
                        if m >= 4:
                            dve.wait_ge(nlo_done, DC * tnum[k] + m - 3)
                        nc.vector.scalar_tensor_tensor(out=tn[:, m % 4], in0=hT[:, m], scalar=norm_gain(k, m),
                                                       in1=rstd[:, :], op0=ALU.mult, op1=ALU.mult).then_inc(t_done, 1)
                    if m > 0 and k != 3:
                        n = m - 1
                        dve.wait_ge(nhi_done, DC * tnum[k] + n + 1)
                        nc.vector.scalar_tensor_tensor(out=nlo[:, n], in0=tn[:, n % 4], scalar=norm_shift(k, n),
                                                       in1=nhi[:, n].bitcast(F32), op0=ALU.add,
                                                       op1=ALU.subtract).then_inc(nlo_done, 1)

            def reduce_products(a, reps=None):
                add = reps if reps is not None else 0
                dve.wait_ge(aprod_done if by_act(a) else prod_done, products(a, by_act(a)) + add)
                slot = a % 2 if a < MOD_START else ADA_SLOT[a]
                last = max([n for n in range(a) if (n % 2 if n < MOD_START else ADA_SLOT[n]) == slot], default=-1)
                if last >= 0:
                    dve.wait_ge(mod_cols, last + 1 + add)
                src = start_slots[a % 5] if a < MOD_START else ada[:, slot]
                nc.vector.tensor_reduce(macc[:, slot], src.rearrange("p c n -> p n c"), AX_X,
                                        ALU.add).then_inc(macc_done, 1)

            def mod_out(a, count=2, reps=None):
                n = 2 * count
                dve.wait_ge(mod_cols, a + count + (reps if reps is not None else 0))
                ps = mod0_ps if a == 0 else (mod2_ps if 19 <= a < 32 and reps is None or a == 34 else mod1_ps)[:, 0:n]
                at = 2 * a if reps is None else reps * 2 + 2 * a
                nc.vector.tensor_tensor(mod[:, bass.ds(at, n)], ps, biasT[:, bass.ds(at, n)],
                                        ALU.add).then_inc(mod_done, count)

            def coefficient(k):
                return nc.vector.scalar_tensor_tensor(
                    out=coefA[:, k], in0=mod[:, 24 * k + 8:24 * k + 16], scalar=1.0,
                    in1=gainT[:, gain_col[k]:gain_col[k] + 8], op0=ALU.add, op1=ALU.mult)

            def job(st):
                if st["kind"] == "W":
                    dve.wait_ge(yhi_done, st["y"] + 1)
                    i = st["i"]
                    nc.vector.tensor_tensor(ylo[:, 2 * i:2 * i + 2], kraw[:, :, :], yhi[:, 2 * i:2 * i + 2].bitcast(F32),
                                            ALU.subtract).then_inc(ylo_done, 1)
                elif st["kind"] == "Q" and st["next"]["kind"] in ("TPV", "ROTK") or st["next"]["kind"] == "SC":
                    pass
                else:
                    low(st["u"] + NS)

            def rope(st):
                one = st["mixer"] == "window" and st["kind"] == "ROTK"
                dve.wait_ge(job_out, st["p"] + 1)
                if st["r"]:
                    dve.wait_ge(rope_done, st["r"])
                if one:
                    src, ps = kraw[:, 0], rot_ps[:, 0:S]
                    a, b, to, co, si = rope_c[:, 0], rope_s[:, 0], kraw[:, 0], cos1, sin1
                else:
                    src = kraw[:, :, :] if st["kind"] == "ROTK" else qraw[:, :, :]
                    ps = rot_ps[:, :].rearrange("p (b n) -> p b n", b=2)
                    a, b, co, si = rope_c, rope_s, cos2, sin2
                    to = kraw[:, :, :] if st["kind"] == "ROTK" else qT[:, :, :]
                nc.vector.tensor_tensor(a, src, co, ALU.mult).then_inc(dve_step, 1)
                dve.wait_ge(rot_done, st["r"] + 1)
                steps[0] += 1
                link(nc.vector.tensor_tensor(b, ps, si, ALU.mult))
                nc.vector.tensor_tensor(to, a, b, ALU.add).then_inc(rope_done, 1)

            def masked_max(st, n):
                h = st["h"] + n
                s = h % 4
                dve.wait_ge(sc_done, h + 1)
                if st["mixer"] == "pool":
                    dve.wait_ge(alibi_done, h + 1)
                    mask = alibi[:, h % 2]
                else:
                    at = C_WIN if st["mixer"] == "window" else C_CAUSAL
                    mask = consts[:, at:at + SW]
                for b, (lo, up) in enumerate(((0, P), (P, SW))):
                    ins = nc.vector.tensor_tensor_reduce(out=prob[:, s, lo:up], in0=sc[h % 2][:, lo:up],
                                                         in1=mask[:, lo:up], scale=1.0, scalar=NEG,
                                                         op0=ALU.add, op1=ALU.max, accum_out=mx[:, s, b:b + 1])
                ins.then_inc(sm_read, 1)
                dve.wait_ge(sm_read, h + 1)
                if st["mixer"] == "window":
                    head = st["local"] + n
                    nc.vector.tensor_scalar(nm[:, s], mx[:, s], sinks[:, head:head + 1], -1.0, ALU.max,
                                            ALU.mult).then_inc(nm_done, 1)
                else:
                    nc.vector.tensor_scalar(nm[:, s], mx[:, s], -1.0, None, ALU.mult).then_inc(nm_done, 1)

            def divide(st, n):
                h = st["h"] + n
                s = h % 4
                dve.wait_ge(ex_done, h + 1)
                if st["mixer"] == "window":
                    link(nc.vector.tensor_tensor(den[:, s], den[:, s], esink[:, s], ALU.add))
                link(nc.vector.reciprocal(rden[:, s], den[:, s]))
                for b, (lo, up) in enumerate(((0, P), (P, SW))):
                    ins = nc.vector.tensor_scalar(prob[:, s, lo:up], prob[:, s, lo:up], rden[:, s, b:b + 1], None,
                                                  ALU.mult)
                ins.then_inc(p_done, 1)

            def outputs(st):
                for n in range(2):
                    g = st["g"] + n
                    dve.wait_ge(pv_done, g + 1)
                    dve.wait_ge(ylo_done, st["y"] + n - 1)
                    o = o_ps[n][:, 0:S]
                    if st["mixer"] == "pool":
                        ins = nc.vector.tensor_copy(og[:, g % 2], o)
                    else:
                        ins = nc.vector.scalar_tensor_tensor(out=og[:, g % 2], in0=o, scalar=0.5, in1=sz[:, n],
                                                             op0=ALU.mult, op1=ALU.mult)
                    ins.then_inc(og_done, 1)
                    ch = y_chunk(st, n)
                    dve.wait_ge(yhi_done, st["y"] + n + 1)
                    nc.vector.tensor_tensor(ylo[:, ch], og[:, g % 2], yhi[:, ch].bitcast(F32),
                                            ALU.subtract).then_inc(ylo_done, 1)

            def mixer(name):
                before, query = None, None
                for st in PLANS[name]:
                    kind = st["kind"]
                    if kind == "Q":
                        query = st
                    if st.get("job"):
                        job(st)
                    elif kind in ("ROTK", "ROTQ"):
                        rope(st)
                        if kind == "ROTQ":
                            low(query["u"] + NS)
                    elif kind == "SC":
                        masked_max(st, 0)
                        masked_max(st, 1)
                        if before["kind"] == "Z":
                            gate(before)
                        divide(st, 0)
                        masked_max(st, 2)
                        divide(st, 1)
                        masked_max(st, 3)
                        divide(st, 2)
                        divide(st, 3)
                        low(before["u"] + NS) if before["kind"] in ("Z", "V") else None
                    elif kind == "TPV":
                        outputs(st)
                        if name == "pool" and before["kind"] == "Q":
                            low(before["u"] + NS)
                    elif kind in ("OUTB", "OUT"):
                        if name != "causal":
                            residual(MIX_NORM[name] + 1, range(2 * st["i"], 2 * st["i"] + 2))
                        if st["i"] < 3 or name == "causal":
                            low(st["u"] + NS)
                    elif kind == "MAC":
                        reduce_products(st["i"])
                        reduce_products(st["i"] + 1)
                    elif kind == "MOD":
                        mod_out(st["i"])
                    before = st

            def gate(st):
                dve.wait_ge(job_out, st["p"] + 1)
                pair = acc[st["p"] % 2][:, :].rearrange("p (b n) -> p b n", b=2)
                nc.vector.scalar_tensor_tensor(out=sz[:, :, :], in0=sz[:, :, :], scalar=1.0, in1=pair, op0=ALU.add,
                                               op1=ALU.mult).then_inc(z_done, 1)

            def ffn(f):
                base, n0 = FFN_UNIT[f], FB * f
                done = (FB * 3 - 1) * f
                up_ps = sc[1][:, :].rearrange("p (b n) -> p b n", b=2)

                def hidden_product(i, reps=None):
                    add = reps if reps is not None else 0
                    dve.wait_ge(silu_done, n0 + i + 1 + add)
                    if n0 + i > 0:
                        dve.wait_ge(hlo_done, n0 + i + add)
                    nc.vector.tensor_tensor(hidden, silu_g, up_ps, ALU.mult).then_inc(hid_done, 1)

                def hidden_low(i, reps=None):
                    dve.wait_ge(hhi_done, n0 + i + 1 + (reps if reps is not None else 0))
                    nc.vector.tensor_tensor(hlo[:, :, :], hidden, hhi[:, :, :].bitcast(F32),
                                            ALU.subtract).then_inc(hlo_done, 1)

                low(base + 3)
                dve.wait_ge(ffn_used, done + 2)
                hidden_product(0)
                low(base + 4)
                hidden_low(0)
                if f == 0:
                    reduce_products(9)
                    mod_out(8, 1)
                for start, end in ((0, FB - 1),) if f == 0 else ((0, 2), (2, 6), (6, FB - 1)):
                    with dve.Fori(start, end) as j:
                        u = base + 2
                        low(u + 3, reps=j)
                        dve.wait_ge(ffn_used, 3 * j + (done + 4))
                        hidden_product(1, reps=j)
                        low(u + 4, reps=j)
                        hidden_low(1, reps=j)
                        low(u + 5, reps=j)
                        if f == 0:
                            mod_out(9, 1, reps=j)
                            reduce_products(10, reps=j)
                    if end == 2:
                        reduce_products(32)
                        reduce_products(33)
                    elif end == 6:
                        mod_out(32)
                        reduce_products(34)
                        reduce_products(35)
                if f == 1:
                    mod_out(34)
                    dve.wait_ge(mod_done, MOD_UNITS)
                    link(nc.vector.tensor_scalar(gate_h[:, 1], mod[:, 64:72], 0.5, None, ALU.mult))
                else:
                    dve.wait_ge(mod_done, 19)
                    link(nc.vector.tensor_scalar(gate_h[:, 0], mod[:, 16:24], 0.5, None, ALU.mult))
                residual(FFN_NORM[f] + 1)
                if f == 0:
                    mod_out(19, 1)
                    dve.wait_ge(mod_done, 20)
                    link(coefficient(1))

            nc.vector.memset(tiny[:, 0:1], EPS1)
            nc.vector.memset(tiny[:, 1:2], EPS2)
            nc.vector.memset(tiny[:, 2:3], 0.0).then_inc(set_done, 1)
            dve.wait_ge(rows_t, 2)
            nc.vector.tensor_copy(biasT[:, :], sc[0][:, 0:72]).then_inc(gains_done, 1)
            nc.vector.tensor_copy(gainT[:, :], sc[0][:, 128:188]).then_inc(gains_done, 1)
            dve.wait_ge(c_done, 1)

            for m in range(DC):
                dve.wait_ge(x_t, 2 * (m // 2) + 2)
                nc.vector.tensor_copy(hT[:, m], acc[m // 2][:, (m % 2) * S:(m % 2 + 1) * S]).then_inc(res_done, 1)
            for a in range(MOD_START):
                reduce_products(a)
                if a == 1:
                    inverse_deviation(0)
            mod_out(0, MOD_START)
            dve.wait_ge(mod_done, MOD_START)
            link(coefficient(0))
            normalise(0)
            dve.wait_ge(lo_done, 1)
            low(1)
            low(2)
            reduce_products(8)
            ffn(0)
            normalise(1)
            low(FFN_UNIT[0] + 3 * FB + 2)
            dve.wait_ge(tables_in, 16)
            mixer("pool")
            dve.wait_ge(mod_done, 32)
            link(coefficient(2))
            normalise(2)
            low(FFN_UNIT[1] + 2)
            ffn(1)
            normalise(3)
            low(FFN_UNIT[1] + 3 * FB + 2)
            normalise(4)
            dve.wait_ge(late_in, 32)
            mixer("window")
            normalise(5)
            low(PLANS["causal"][0]["u"] + 2)
            mixer("causal")
            dve.wait_ge(fss_done, 4)
            nc.vector.tensor_reduce(fst[:, 0], fss[:, :, :], AX_X, ALU.add).then_inc(fsum_done, 1)
            dve.wait_ge(fstd_done, 1)
            link(nc.vector.reciprocal(fst[:, 2], fst[:, 1]))
            for j in range(4):
                for b in range(2):
                    ins = nc.vector.scalar_tensor_tensor(
                        out=xo[:, b, j * UC:(j + 1) * UC], in0=acc[j][:, b * S:(b + 1) * S],
                        scalar=fst[:, 2, b:b + 1], in1=fgain[:, j * UC:(j + 1) * UC], op0=ALU.mult, op1=ALU.mult)
                ins.then_inc(res_out, 1)

        @block.tensor
        def _(pe):
            mm = nc.tensor.matmul

            def split_product(to, stat_hi, stat_lo, mov_hi, mov_lo, first, last):
                mm(to, stat_hi, mov_hi, start=first, stop=False, skip_group_check=True)
                mm(to, stat_hi, mov_lo, start=False, stop=False, skip_group_check=True)
                return mm(to, stat_lo, mov_hi, start=False, stop=last, skip_group_check=True)

            def sum_squares(k, m, first, last=False):
                if m is None:
                    pe.wait_ge(sqs_done, 3 * k)
                else:
                    pe.wait_ge(sq_done, DC * k + m + 1)
                src = std[:, :] if m is None else sq[:, m % 4]
                mm(ss_ps, ones[:, :], src, start=first, stop=last).then_inc(ss_done, 1)

            def sums_within(k, n):
                if n == 6:
                    sum_squares(k, None, True)
                elif n == 7:
                    sum_squares(k, 4, False)
                    sum_squares(k, 5, False)

            def sums_after(k):
                sum_squares(k, 6, False)
                sum_squares(k, 7, False, True)

            def mod_sum(a, to, reps=None):
                pe.wait_ge(macc_done, a + 1 + (reps if reps is not None else 0))
                slot = a % 2 if a < MOD_START else ADA_SLOT[a]
                for n in range(2):
                    ins = mm(to[:, n:n + 1], macc[:, slot, n * P:(n + 1) * P], ones[:, 0:1],
                             start=True, stop=True)
                ins.then_inc(mod_cols, 1)

            def project(bank, slot, k=None, chunks=(0, 1)):
                hi, lo = rows8(whi, slot), rows8(wlo, slot)
                order = [(m, ch) for m in chunks for ch in range(DC)]
                if k is not None:
                    order = [(m, ch) for ch in range(DC) for m in chunks]
                for m, ch in order:
                    if k is not None and m == 0:
                        pe.wait_ge(nlo_done, DC * tnum[k] + ch + 1)
                    at = slice(m * P, (m + 1) * P)
                    ins = split_product(bank[:, m * S:(m + 1) * S], hi[:, ch, at], lo[:, ch, at],
                                        nhi[:, ch], nlo[:, ch], ch == 0 and (k is None or m == 0), ch == DC - 1)
                return ins

            def project_rows(bank, slot, col, width, at0):
                hi, lo = rows8(whi, slot), rows8(wlo, slot)
                for b in range(2):
                    for ch in range(DC):
                        tok = slice(b * P, (b + 1) * P)
                        to = bank[:, at0 + b * width:at0 + (b + 1) * width]
                        w = slice(col, col + width)
                        mm(to, nhi[:, ch, tok], hi[:, ch, w], start=(ch == 0), stop=False, skip_group_check=True)
                        mm(to, nhi[:, ch, tok], lo[:, ch, w], start=False, stop=False, skip_group_check=True)
                        ins = mm(to, nlo[:, ch, tok], hi[:, ch, w], start=False, stop=(ch == DC - 1),
                                 skip_group_check=True)
                return ins

            def job(st):
                kind, p = st["kind"], st["p"]
                if p >= 2:
                    pe.wait_ge(job_out, p - 1)
                if st["zs"]:
                    pe.wait_ge(z_done, st["zs"])
                bank = acc[p % 2]
                if kind == "W":
                    pe.wait_ge(pooled, 2 * st["i"] + 2)
                    pe.wait_ge(wpool_in, 16)
                    for n in range(2):
                        g = 2 * st["i"] + n
                        ins = mm(bank[:, n * S:(n + 1) * S], wpool[:, g], tmp[:, g, 8:8 + S], start=True, stop=True)
                    ins.then_inc(job_done, 1)
                    return
                u = st["u"]
                pe.wait_ge(lo_done, u + 1)
                k = MIX_NORM[st["mixer"]] if st["first"] else None
                if kind == "V" and st["next"]["kind"] == "SC":
                    scores(st["next"], (0, 1))
                if kind == "V":
                    ins = project_rows(bank, u % NS, 0, UC, 0)
                elif kind == "KV":
                    project(bank, u % NS, k, chunks=(0,))
                    ins = project_rows(bank, u % NS, P, P, S)
                elif kind == "Q" and st["next"]["kind"] == "TPV":
                    project(bank, u % NS, chunks=(0,))
                    transposes(st["next"], 0)
                    transposes(st["next"], 1)
                    ins = project(bank, u % NS, chunks=(1,))
                elif kind == "Z":
                    project(bank, u % NS, chunks=(0,))
                    scores(st["next"], (0, 1))
                    ins = project(bank, u % NS, chunks=(1,))
                else:
                    ins = project(bank, u % NS, k)
                ins.then_inc(job_done, 1)

            def rotate(st):
                pe.wait_ge(job_out, st["p"] + 1)
                if st["r"]:
                    pe.wait_ge(rope_done, st["r"])
                if st["h_before"]:
                    pe.wait_ge(pt_done, st["h_before"])
                if st["kind"] == "ROTK" and st["mixer"] == "window":
                    mm(rot_ps[:, 0:S], rotation, kraw[:, 0], start=True, stop=True).then_inc(rot_done, 1)
                else:
                    src = kraw if st["kind"] == "ROTK" else qraw
                    mm(rot_ps[:, :], rotation, src[:, :, :].rearrange("p b n -> p (b n)"), start=True,
                       stop=True).then_inc(rot_done, 1)

            def scores(st, heads):
                if st["mixer"] == "pool":
                    pe.wait_ge(job_out, st["q"] + 1)
                    pe.wait_ge(mod_done, st["mods"])
                else:
                    pe.wait_ge(rope_done, st["rots"])
                    pe.wait_ge(kd_done, 1 if st["mixer"] == "window" else 2)
                for n in heads:
                    h = st["h"] + n
                    half, kv, _ = head_place(st["mixer"], st["local"] + n)
                    if h >= 2:
                        pe.wait_ge(sm_read, h - 1)
                    part = slice(64 * half, 64 * half + 64)
                    mm(sc[h % 2][:, 0:P], qT[part, n // 2, 0:P], kd[part, kv, 0:P], start=True, stop=True)
                    mm(sc[h % 2][:, P:SW], qT[part, n // 2, P:S], kd[part, kv, :], start=True,
                       stop=True).then_inc(sc_done, 1)

            def transposes(st, n):
                h = st["h"] + n
                pe.wait_ge(p_done, h + 1)
                if h >= 2:
                    pe.wait_ge(pt_done, h - 1)
                for i in range(3):
                    ins = nc.tensor.transpose(tp[h % 2][:, i * P:(i + 1) * P], prob[:, h % 4, i * P:(i + 1) * P], ident)
                ins.then_inc(tp_done, 1)

            def values(st, n):
                h, g = st["h"] + n, st["g"] + n // 2
                half, _, col = head_place(st["mixer"], st["local"] + n)
                pe.wait_ge(pt_done, h + 1)
                if n % 2 == 0 and g >= 2:
                    pe.wait_ge(og_done, g - 1)
                part = slice(64 * half, 64 * half + 64)
                to = o_ps[n // 2]
                mm(to[part, 0:S], vv[:, 0, col:col + HD], probT[:, h % 2, 0:S], start=True, stop=False,
                   skip_group_check=True)
                ins = mm(to[part, P:S], vv[:, 1, col:col + HD], probT[:, h % 2, S:SW], start=False,
                         stop=True, skip_group_check=True)
                if n % 2:
                    ins.then_inc(pv_done, 1)

            def attend(st, early):
                if not early:
                    transposes(st, 0)
                    transposes(st, 1)
                values(st, 0)
                transposes(st, 2)
                values(st, 1)
                transposes(st, 3)
                values(st, 2)
                values(st, 3)

            def y_ready(st, ch):
                pe.wait_ge(ylo_done, st["first_y"] + (ch // 2 + 1 if ch < 4 else ch - 1)
                           if st["mixer"] == "pool" else st["first_y"] + ch + 1)

            def out_product(st, j, m, chunks, first, last):
                hi, lo = rows8(whi, st["u"] % NS), rows8(wlo, st["u"] % NS)
                at = slice(m * P, (m + 1) * P)
                for ch in chunks:
                    if j == 0 and m == 0:
                        y_ready(st, ch)
                    ins = split_product(acc[j % 2][:, m * S:(m + 1) * S], hi[:, ch, at], lo[:, ch, at], yhi[:, ch],
                                        ylo[:, ch], first and ch == chunks[0], last and ch == chunks[-1])
                return ins

            def out_rows(st, j, b, chunks, last):
                hi, lo = rows8(whi, st["u"] % NS), rows8(wlo, st["u"] % NS)
                tok = slice(b * P, (b + 1) * P)
                to = acc[j][:, b * S:(b + 1) * S]
                for ch in chunks:
                    if j == 0 and b == 0:
                        y_ready(st, ch)
                    mm(to, yhi[:, ch, tok], hi[:, ch], start=False, stop=False, skip_group_check=True)
                    mm(to, yhi[:, ch, tok], lo[:, ch], start=False, stop=False, skip_group_check=True)
                    ins = mm(to, ylo[:, ch, tok], hi[:, ch], start=False, stop=last and ch == chunks[-1],
                             skip_group_check=True)
                return ins

            def residual_rows(j):
                for b in range(2):
                    for n in range(2):
                        at = b * S + n * P
                        mm(acc[j][:, at:at + P], hT[:, 2 * j + n, b * P:(b + 1) * P], ident,
                           start=(b == 0 and n == 0), stop=False, skip_group_check=True)

            def out_step(st, before):
                kind, last_layer = st["kind"], st["mixer"] == "causal"
                j = st["i"]
                k = MIX_NORM[st["mixer"]] + 1
                early, late = range(0, 6), range(6, 8)
                if kind in ("OUTA", "OUT"):
                    pe.wait_ge(lo_done, st["u"] + 1)
                    pe.wait_ge(job_out, st["jobs"])
                    if st["zs_all"]:
                        pe.wait_ge(z_done, st["zs_all"])
                if last_layer:
                    if kind == "OUTA":
                        residual_rows(0)
                        residual_rows(1)
                        out_rows(st, 0, 0, early, False)
                        out_rows(st, 0, 1, early, False)
                        return
                    if kind == "OUTB":
                        out_rows(st, 0, 0, late, True)
                        ins = out_rows(st, 0, 1, late, True)
                    else:
                        if j >= 2:
                            residual_rows(j)
                        out_rows(st, j, 0, range(DC), True)
                        ins = out_rows(st, j, 1, range(DC), True)
                    ins.then_inc(fin_mm, 1)
                    return
                if kind == "OUTA":
                    out_product(st, 0, 0, early, True, False)
                    if st["mixer"] == "pool":
                        scores(before, (2, 3))
                    out_product(st, 0, 1, early, False, False)
                    return
                if kind == "OUTB":
                    out_product(st, 0, 0, late, False, True).then_inc(delta, 1)
                    out_product(st, 0, 1, late, False, True).then_inc(delta, 1)
                else:
                    if j >= 2:
                        pe.wait_ge(res_done, DC * k + 2 * (j - 1))
                    for m in range(2):
                        out_product(st, j, m, range(DC), True, True).then_inc(delta, 1)
                        sums_within(k, 2 * j + m)

            def mixer(name):
                before = None
                for st in PLANS[name]:
                    kind = st["kind"]
                    if st.get("job"):
                        job(st)
                    elif kind in ("ROTK", "ROTQ"):
                        rotate(st)
                    elif kind == "SC":
                        if st["next"]["kind"] == "OUTA" and name == "pool":
                            scores(st, (0, 1))
                        else:
                            scores(st, (2, 3) if before["kind"] in ("Z", "V") else range(4))
                    elif kind == "TPV":
                        attend(st, before["kind"] == "Q")
                    elif kind in ("OUTA", "OUTB", "OUT"):
                        out_step(st, before)
                    elif kind == "MOD":
                        if st["h"]:
                            pe.wait_ge(sm_read, st["h"])
                        mod_sum(st["i"], mod2_ps[:, 0:2])
                        mod_sum(st["i"] + 1, mod2_ps[:, 2:4])
                    before = st

            def ffn(f):
                base, n0, k = FFN_UNIT[f], FB * f, FFN_NORM[f]

                def gate(u, i, reps=None, norm=None):
                    add = reps if reps is not None else 0
                    pe.wait_ge(lo_done, u + 1 + 3 * add)
                    if n0 + i > 0:
                        pe.wait_ge(silu_done, n0 + i + add)
                    project(sc[0], u % NS, norm).then_inc(ffn_used, 1)

                def up(u, i, reps=None):
                    add = reps if reps is not None else 0
                    pe.wait_ge(lo_done, u + 1 + 3 * add)
                    if n0 + i > 0:
                        pe.wait_ge(hid_done, n0 + i + add)
                    project(sc[1], u % NS).then_inc(ffn_used, 1)

                def down(u, i, reps=None):
                    add = reps if reps is not None else 0
                    hi, lo = rows2(whi, u % NS), rows2(wlo, u % NS)
                    pe.wait_ge(lo_done, u + 1 + 3 * add)
                    pe.wait_ge(hlo_done, n0 + i + 1 + add)
                    for m in range(DC):
                        for n in range(2):
                            at = slice(m * P, (m + 1) * P)
                            ins = split_product(acc[m // 2][:, (m % 2) * S:(m % 2 + 1) * S], hi[:, n, at], lo[:, n, at],
                                                hhi[:, n], hlo[:, n], False, False)
                        yield m, ins

                gate(base, 0, norm=k)
                up(base + 1, 0)
                for bank in acc:
                    mm(bank[:, :], zero_r[:, 0:P], zero_r[:, :], start=True, stop=False, skip_group_check=True)
                if f == 0:
                    mod_sum(8, mod1_ps[:, 0:2])
                for start, end in ((0, FB - 1),) if f == 0 else ((0, 3), (3, FB - 1)):
                    with pe.Fori(start, end) as j:
                        gate(base + 2, 1, reps=j)
                        up(base + 3, 1, reps=j)
                        for m, ins in down(base + 4, 0, reps=j):
                            if m == DC - 1:
                                ins.then_inc(ffn_used, 1)
                        if f == 0:
                            pe.wait_ge(mod_done, 9 + j)
                            mod_sum(9, mod1_ps[:, 0:2], reps=j)
                    if end == 3:
                        mod_sum(32, mod1_ps[:, 0:2])
                        mod_sum(33, mod1_ps[:, 2:4])
                for m, ins in down(base + 32, FB - 1):
                    ins.then_inc(delta, 1)
                    if f == 0 and m == 5:
                        mod_sum(19, mod2_ps[:, 0:2])
                    if f == 1 and m == 1:
                        mod_sum(34, mod2_ps[:, 0:2])
                        mod_sum(35, mod2_ps[:, 2:4])
                    sums_within(k + 1, m)
                sums_after(k + 1)

            pe.wait_ge(consts_in, 16)
            pe.wait_ge(rows_in, 128)
            nc.tensor.transpose(sc[0][:, 0:72], rowsA, ident[0:72, 0:72]).then_inc(rows_t, 1)
            nc.tensor.transpose(sc[0][:, 128:188], rowsB, ident[0:60, 0:60]).then_inc(rows_t, 1)
            pe.wait_ge(x_in, 16)
            for m in range(DC):
                for b in range(2):
                    at = (m % 2) * S + b * P
                    ins = nc.tensor.transpose(acc[m // 2][:, at:at + P], xo[:, b, m * P:(m + 1) * P], ident)
                ins.then_inc(x_t, 1)
            pe.wait_ge(set_done, 4)
            for m in range(DC):
                sum_squares(0, m, m == 0, m == DC - 1)
            for a in range(MOD_START):
                mod_sum(a, mod0_ps[:, 2 * a:2 * a + 2])
            ffn(0)
            pe.wait_ge(tables_in, 16)
            mixer("pool")
            sums_after(2)
            ffn(1)
            for n, m in enumerate((4, 5, 6, 7, None)):
                sum_squares(4, m, n == 0, n == 4)
            mixer("window")
            sums_after(5)
            mixer("causal")


tnum = {0: 0, 1: 1, 2: 2, 4: 3, 5: 4}
z_pairs = {"window": 4, "causal": 12}


def y_chunk(st, n):
    return st["local"] // 2 + n + (4 if st["mixer"] == "pool" else 0)


def heads_before_rotations():
    done = 0
    for name in ("pool", "window", "causal"):
        for st in PLANS[name]:
            if st["kind"] == "TPV":
                done = st["h"] + 4
            elif st["kind"] in ("ROTK", "ROTQ"):
                st["h_before"] = done


heads_before_rotations()

_INS = ["x", "c", "w_ada", "b_ada", "g_ffn1", "w1_gate", "w1_up", "w1_down", "g_mix", "w_in", "w_pool",
        "pool_scale", "w_out", "g_ffn2", "w2_gate", "w2_up", "w2_down", "g_final", "norm_g_2", "w_in_a_2",
        "sinks_a_2", "w_in_b_2", "w_out_2", "final_g_2"]


def kernel(**inputs):
    import concourse.bacc as _bacc
    from concourse.bass_utils import run_bass_kernel_spmd as _run

    nc = _bacc.Bacc("TRN2", target_bir_lowering=False, num_devices=1)
    arrays, args = {}, []
    for name in _INS:
        a = np.ascontiguousarray(inputs[name])
        arrays[f"in_{name}_dram"] = a
        args.append(nc.dram_tensor(f"in_{name}_dram", a.shape, mybir.dt.from_np(a.dtype), kind="ExternalInput").ap())
    arrays["shape_consts_dram"] = shape_constants()
    args.append(nc.dram_tensor("shape_consts_dram", (P, C_END), F32, kind="ExternalInput").ap())
    out = nc.dram_tensor("out_0_dram", (1, S, D), F32, kind="ExternalOutput").ap()
    build(nc, *args, out)
    r = _run(nc, [arrays], core_ids=[0])
    return r.results[0]["out_0_dram"]
```
